# Optimizing a Trainium2 kernel written in Bass

```python
import jax, jax.numpy as jnp
from jax import lax
import numpy as np

D_MODEL = 1024
BATCH = 1
SEQ = 256
DEPTH = 2

GM_GROUPS = 4
GM_DIM = 256
GM_CHUNK = 128
GM_WIDTH = GM_GROUPS * GM_DIM
RET_HEADS = 4
RET_QK_DIM = 128
RET_V_DIM = 256
RET_CHUNK = 128
RET_QK_WIDTH = RET_HEADS * RET_QK_DIM
RET_V_WIDTH = RET_HEADS * RET_V_DIM
HY_SPLITS = [GM_WIDTH, 2 * GM_WIDTH, 2 * GM_WIDTH + RET_QK_WIDTH,
             2 * GM_WIDTH + 2 * RET_QK_WIDTH, 2 * GM_WIDTH + 2 * RET_QK_WIDTH + RET_V_WIDTH]
HY_IN_WIDTH = 2 * GM_WIDTH + 2 * RET_QK_WIDTH + 2 * RET_V_WIDTH
HY_OUT_WIDTH = GM_WIDTH + RET_V_WIDTH
MLA_HEADS = 8
MLA_Q_RANK = 384
MLA_KV_RANK = 256
MLA_NOPE_DIM = 128
MLA_ROPE_DIM = 64
MLA_V_DIM = 128
MLA_QK_DIM = MLA_NOPE_DIM + MLA_ROPE_DIM
MLA_DOWN_WIDTH = MLA_Q_RANK + MLA_KV_RANK + MLA_ROPE_DIM
Q_BLOCK = 128
ROPE_THETA = 10000.0
PEER_HEADS = 8
PEER_N_KEYS = 128
PEER_N_EXPERTS = PEER_N_KEYS * PEER_N_KEYS
PEER_QUERY_DIM = 256
PEER_HALF = PEER_QUERY_DIM // 2
PEER_TOPK = 16
PEER_TOKEN_BLOCK = 128
NORM_EPS = 1e-6

kernel_name = "gmlp_retention_mla_peer_hybrid"

def rmsnorm(x, g):
    xf = x.astype(jnp.float32)
    y = xf * lax.rsqrt(jnp.mean(xf * xf, axis=-1, keepdims=True) + NORM_EPS)
    return (y * g.astype(jnp.float32)).astype(x.dtype)

def rope(x):
    s, d = x.shape[1], x.shape[-1]
    half = d // 2
    inv = 1.0 / (ROPE_THETA ** (jnp.arange(half, dtype=jnp.float32) / half))
    ang = jnp.arange(s, dtype=jnp.float32)[:, None] * inv[None, :]
    cos = jnp.cos(ang)[None, :, None, :]
    sin = jnp.sin(ang)[None, :, None, :]
    xf = x.astype(jnp.float32)
    x1, x2 = xf[..., :half], xf[..., half:]
    return jnp.concatenate([x1 * cos - x2 * sin, x1 * sin + x2 * cos], axis=-1).astype(x.dtype)

def chunk_gating_mlp(u, v, v_norm, w_s, b_s):
    b, s, _ = u.shape
    nc = s // GM_CHUNK
    v = rmsnorm(v.reshape(b, s, GM_GROUPS, GM_DIM), v_norm.reshape(GM_GROUPS, GM_DIM))
    v = v.reshape(b, nc, GM_CHUNK, GM_GROUPS, GM_DIM)
    causal = jnp.tril(jnp.ones((GM_CHUNK, GM_CHUNK), dtype=bool))
    w = jnp.where(causal[None], w_s, 0.0).astype(v.dtype)
    mixed = jnp.einsum('gts,bnsgd->bntgd', w, v) + jnp.transpose(b_s)[None, None, :, :, None]
    return u * mixed.reshape(b, s, GM_WIDTH)

def retention(q, k, v):
    b, s, h, dk = q.shape
    dv = v.shape[-1]
    c = RET_CHUNK
    nc = s // c
    log_gamma = jnp.log(1.0 - 2.0 ** (-5.0 - jnp.arange(h, dtype=jnp.float32)))
    pos = jnp.arange(c, dtype=jnp.float32)
    diff = pos[:, None] - pos[None, :]
    decay_mask = jnp.where(diff[None] >= 0, jnp.exp(diff[None] * log_gamma[:, None, None]), 0.0)
    q_decay = jnp.exp((pos[:, None] + 1.0) * log_gamma[None, :])
    k_decay = jnp.exp((c - 1.0 - pos[:, None]) * log_gamma[None, :])
    chunk_decay = jnp.exp(c * log_gamma)
    qf = q.astype(jnp.float32).reshape(b, nc, c, h, dk)
    kf = k.astype(jnp.float32).reshape(b, nc, c, h, dk) * (dk ** -0.5)
    vf = v.astype(jnp.float32).reshape(b, nc, c, h, dv)
    scores = jnp.einsum('bnihd,bnjhd->bnhij', qf, kf) * decay_mask[None, None]
    intra = jnp.einsum('bnhij,bnjhe->bnihe', scores, vf)

    def step(state, inp):
        qc, kc, vc = inp
        cross = jnp.einsum('bchd,bhde->bche', qc, state) * q_decay[None, :, :, None]
        state = state * chunk_decay[None, :, None, None] + jnp.einsum(
            'bchd,bche->bhde', kc, vc * k_decay[None, :, :, None])
        return state, cross

    init = jnp.zeros((b, h, dk, dv), jnp.float32)
    _, cross = lax.scan(step, init, (jnp.moveaxis(qf, 1, 0), jnp.moveaxis(kf, 1, 0), jnp.moveaxis(vf, 1, 0)))
    out = intra + jnp.moveaxis(cross, 0, 1)
    return out.reshape(b, s, h, dv).astype(v.dtype)

def gmlp_retention_mixer(h, w_in, gm_v_norm, gm_w_s, gm_b_s, ret_norm, w_out):
    b, s, _ = h.shape
    proj = h @ w_in
    a_u, a_v, r_q, r_k, r_v, r_g = jnp.split(proj, HY_SPLITS, axis=-1)
    y_a = chunk_gating_mlp(jax.nn.gelu(a_u, approximate=False), jax.nn.gelu(a_v, approximate=False),
                           gm_v_norm, gm_w_s, gm_b_s)
    q = rope(r_q.reshape(b, s, RET_HEADS, RET_QK_DIM))
    k = rope(r_k.reshape(b, s, RET_HEADS, RET_QK_DIM))
    y_b = retention(q, k, r_v.reshape(b, s, RET_HEADS, RET_V_DIM))
    y_b = rmsnorm(y_b, ret_norm.reshape(RET_HEADS, RET_V_DIM)).reshape(b, s, RET_V_WIDTH)
    y_b = jax.nn.silu(r_g) * y_b
    return jnp.concatenate([y_a, y_b], axis=-1) @ w_out

def causal_block_attention(q, k, v):
    b, s, h, d = q.shape
    dv = v.shape[-1]
    nb = s // Q_BLOCK
    scale = d ** -0.5
    qb = jnp.moveaxis(q.reshape(b, nb, Q_BLOCK, h, d), 1, 0)
    k_pos = jnp.arange(s)

    def one_block(inp):
        q_blk, i = inp
        scores = jnp.einsum('bqhd,bkhd->bhqk', q_blk, k).astype(jnp.float32) * scale
        q_pos = i * Q_BLOCK + jnp.arange(Q_BLOCK)
        mask = k_pos[None, :] <= q_pos[:, None]
        scores = jnp.where(mask[None, None], scores, -jnp.inf)
        p = jax.nn.softmax(scores, axis=-1).astype(v.dtype)
        return jnp.einsum('bhqk,bkhe->bqhe', p, v)

    out = lax.map(one_block, (qb, jnp.arange(nb)))
    return jnp.moveaxis(out, 0, 1).reshape(b, s, h, dv)

def mla(h, w_down, q_norm, w_q_up, kv_norm, w_kv_up, w_out):
    b, s, _ = h.shape
    down = h @ w_down
    c_q, c_kv, k_rope = jnp.split(down, [MLA_Q_RANK, MLA_Q_RANK + MLA_KV_RANK], axis=-1)
    q = (rmsnorm(c_q, q_norm) @ w_q_up).reshape(b, s, MLA_HEADS, MLA_QK_DIM)
    q = jnp.concatenate([q[..., :MLA_NOPE_DIM], rope(q[..., MLA_NOPE_DIM:])], axis=-1)
    kv = (rmsnorm(c_kv, kv_norm) @ w_kv_up).reshape(b, s, MLA_HEADS, MLA_NOPE_DIM + MLA_V_DIM)
    k_nope, v = kv[..., :MLA_NOPE_DIM], kv[..., MLA_NOPE_DIM:]
    k_rope = rope(k_rope[:, :, None, :])
    k = jnp.concatenate([k_nope, jnp.broadcast_to(k_rope, (b, s, MLA_HEADS, MLA_ROPE_DIM))], axis=-1)
    o = causal_block_attention(q, k, v)
    return o.reshape(b, s, MLA_HEADS * MLA_V_DIM) @ w_out

def peer(h, w_q, sub_keys, u_tab, v_tab):
    b, s, dm = h.shape
    t = b * s
    xt = h.reshape(t, dm)
    qry = (xt @ w_q).reshape(t, PEER_HEADS, 2, PEER_HALF)
    scores = jnp.einsum('thpd,pkd->thpk', qry, sub_keys).astype(jnp.float32)
    top_s, top_i = lax.top_k(scores, PEER_TOPK)
    cand = top_s[:, :, 0, :, None] + top_s[:, :, 1, None, :]
    best_s, best_c = lax.top_k(cand.reshape(t, PEER_HEADS, PEER_TOPK * PEER_TOPK), PEER_TOPK)
    i1 = jnp.take_along_axis(top_i[:, :, 0], best_c // PEER_TOPK, axis=-1)
    i2 = jnp.take_along_axis(top_i[:, :, 1], best_c % PEER_TOPK, axis=-1)
    experts = i1 * PEER_N_KEYS + i2
    gates = jax.nn.softmax(best_s, axis=-1).astype(h.dtype)
    nb = t // PEER_TOKEN_BLOCK

    def block(inp):
        xb, eb, gb = inp
        act = jax.nn.gelu(jnp.einsum('td,thkd->thk', xb, u_tab[eb]), approximate=False)
        return jnp.einsum('thk,thkd->td', gb * act, v_tab[eb])

    out = lax.map(block, (xt.reshape(nb, PEER_TOKEN_BLOCK, dm),
                          experts.reshape(nb, PEER_TOKEN_BLOCK, PEER_HEADS, PEER_TOPK),
                          gates.reshape(nb, PEER_TOKEN_BLOCK, PEER_HEADS, PEER_TOPK)))
    return out.reshape(b, s, dm)

def setup_inputs(seed: int = 0) -> dict:
    key = jax.random.key(seed)
    ks = jax.random.split(key, 24)
    n_even = (DEPTH + 1) // 2
    n_odd = DEPTH // 2
    f32 = jnp.float32

    def nrm(k, shape, scale):
        return jax.random.normal(k, shape, f32) * scale

    def gain(k, shape):
        return 1.0 + 0.01 * jax.random.normal(k, shape, f32)

    return {
        "x": jax.random.normal(ks[0], (BATCH, SEQ, D_MODEL), f32),
        "norm_mix": gain(ks[1], (DEPTH, D_MODEL)),
        "norm_ffn": gain(ks[2], (DEPTH, D_MODEL)),
        "hy_w_in": nrm(ks[3], (n_even, D_MODEL, HY_IN_WIDTH), D_MODEL ** -0.5),
        "gm_v_norm": gain(ks[4], (n_even, GM_WIDTH)),
        "gm_w_s": nrm(ks[5], (n_even, GM_GROUPS, GM_CHUNK, GM_CHUNK), GM_CHUNK ** -0.5),
        "gm_b_s": gain(ks[6], (n_even, GM_GROUPS, GM_CHUNK)),
        "ret_norm": gain(ks[7], (n_even, RET_V_WIDTH)),
        "hy_w_out": nrm(ks[8], (n_even, HY_OUT_WIDTH, D_MODEL), HY_OUT_WIDTH ** -0.5),
        "mla_w_down": nrm(ks[9], (n_odd, D_MODEL, MLA_DOWN_WIDTH), D_MODEL ** -0.5),
        "mla_q_norm": gain(ks[10], (n_odd, MLA_Q_RANK)),
        "mla_w_q_up": nrm(ks[11], (n_odd, MLA_Q_RANK, MLA_HEADS * MLA_QK_DIM), MLA_Q_RANK ** -0.5),
        "mla_kv_norm": gain(ks[12], (n_odd, MLA_KV_RANK)),
        "mla_w_kv_up": nrm(ks[13], (n_odd, MLA_KV_RANK, MLA_HEADS * (MLA_NOPE_DIM + MLA_V_DIM)), MLA_KV_RANK ** -0.5),
        "mla_w_out": nrm(ks[14], (n_odd, MLA_HEADS * MLA_V_DIM, D_MODEL), (MLA_HEADS * MLA_V_DIM) ** -0.5),
        "peer_w_q": nrm(ks[15], (DEPTH, D_MODEL, PEER_HEADS * PEER_QUERY_DIM), D_MODEL ** -0.5),
        "peer_sub_keys": nrm(ks[16], (DEPTH, 2, PEER_N_KEYS, PEER_HALF), PEER_HALF ** -0.5),
        "peer_u": nrm(ks[17], (DEPTH, PEER_N_EXPERTS, D_MODEL), D_MODEL ** -0.5),
        "peer_v": nrm(ks[18], (DEPTH, PEER_N_EXPERTS, D_MODEL), PEER_HEADS ** -0.5),
        "final_norm": gain(ks[19], (D_MODEL,)),
    }

def reference(x, norm_mix, norm_ffn, hy_w_in, gm_v_norm, gm_w_s, gm_b_s, ret_norm, hy_w_out,
              mla_w_down, mla_q_norm, mla_w_q_up, mla_kv_norm, mla_w_kv_up, mla_w_out,
              peer_w_q, peer_sub_keys, peer_u, peer_v, final_norm):
    for layer in range(DEPTH):
        j = layer // 2
        h = rmsnorm(x, norm_mix[layer])
        if layer % 2 == 0:
            x = x + gmlp_retention_mixer(h, hy_w_in[j], gm_v_norm[j], gm_w_s[j], gm_b_s[j],
                                         ret_norm[j], hy_w_out[j])
        else:
            x = x + mla(h, mla_w_down[j], mla_q_norm[j], mla_w_q_up[j], mla_kv_norm[j],
                        mla_w_kv_up[j], mla_w_out[j])
        h = rmsnorm(x, norm_ffn[layer])
        x = x + peer(h, peer_w_q[layer], peer_sub_keys[layer], peer_u[layer], peer_v[layer])
    return rmsnorm(x, final_norm)


_drawn_inputs = setup_inputs


def setup_inputs(seed=0):
    import zlib

    import numpy as np

    out = dict(_drawn_inputs(seed))
    spreads = {}
    factors = {'gm_v_norm': 4.15,
     'gm_b_s': 3.318,
     'ret_norm': 3.299,
     'mla_q_norm': 8.0,
     'mla_kv_norm': 7.599,
     'final_norm': 5.702}
    for name, (base, spread) in spreads.items():
        noise = np.random.default_rng([zlib.crc32(name.encode()), seed]).standard_normal(out[name].shape)
        drawn = base * np.exp(spread * noise) if base else spread * noise
        out[name] = __import__('jax').numpy.asarray(drawn.astype(out[name].dtype))
    for name, factor in factors.items():
        out[name] = (out[name] * factor).astype(out[name].dtype)
    return out
```

```python
from contextlib import ExitStack

import numpy as np

import concourse.bass as bass
from concourse import mybir

ALU = mybir.AluOpType
ACT = mybir.ActivationFunctionType
F32 = mybir.dt.float32
U32 = mybir.dt.uint32
AX = mybir.AxisListType.X

P = 128
D = 1024
KD = D // P
LAYERS, BLOCKS = 2, 2
UNITS = LAYERS * BLOCKS
BANK = 512
EPS = 1e-6

GM_G, GM_D = 4, 256
RH, RQK, RV = 4, 128, 256
QR, KVR = 384, 256
MH, NOPE, ROPE, MV = 8, 128, 64, 128
QKD = NOPE + ROPE
DOWN = QR + KVR + ROPE
ATT_SCALE = QKD ** -0.5
PH, TOPK, NKEYS = 8, 16, 128
N_EXPERTS = NKEYS * NKEYS
PICKS = PH * TOPK

GROUP = 8
GROUPS = PICKS // GROUP
DIAGS = 4
RING = 6
W_SLOTS, W_SIZE = 5, 2048
LOWEST = -3.0e38
MASKED = -1.0e30

IN_ORDER = [4, 5, 2, 3, 0, 1, 6, 7, 8, 9]


def layer_of(u):
    return u // BLOCKS


def block_of(u):
    return u % BLOCKS


def plan_products():
    order = []
    for u in range(UNITS):
        if layer_of(u) == 0:
            names = ["hT0", "hT1"] + [f"in{n}" for n in IN_ORDER] + ["qkT0", "qkT1", "ret_s", "mix0", "mix1",
                                                                     "ret_o0", "ret_o1"]
            if block_of(u) == 0:
                names += ["st0", "st1"]
            names += ["yT0", "yT1", "yT2", "yT3", "out0", "out1"]
        else:
            n = 2 * (block_of(u) + 1)
            names = ["hT0", "hT1", "down0", "down1", "cT0", "cT1", "krT", "qr", "qn0", "qn1", "kn0", "kn1",
                     "v0", "v1", "qrT0", "qrT1"]
            names += [f"s{i}" for i in range(n)] + [f"pT{i}" for i in range(n)]
            names += ["o0", "o1", "oT0", "oT1", "out0", "out1"]
        names += ["fT0", "fT1"] + [f"q{i}" for i in range(4)] + [f"qT{i}" for i in range(4)]
        names += [f"sc{i}" for i in range(4)]
        order += [(u, n) for n in names]
    return {key: i for i, key in enumerate(order)}


PRODUCT = plan_products()


def plan_schedule():
    steps = []
    for u in range(UNITS):
        steps += [("mixer", u), ("route", u), ("picks", u, 0, GROUPS)]
    steps += [("final", 0), ("final", 1)]
    return steps


def build(nc, a, out):
    with ExitStack() as ctx:
        def sb(name, shape, dt=F32):
            return ctx.enter_context(nc.sbuf_tensor(name, shape, dt))

        def sem(name):
            return ctx.enter_context(nc.semaphore(name))

        x = sb("x", [P, BLOCKS, D])
        h = sb("h", [P, 2, D])
        w_ring = sb("w_ring", [P, W_SLOTS, W_SIZE])
        u_rows = sb("u_rows", [P, GROUP, D])
        v_rows = sb("v_rows", [P, GROUP, D])
        work = sb("work", [P, 13, 1024])
        gain_mix = sb("gain_mix", [P, D])
        gain_ffn = sb("gain_ffn", [P, D])
        gm_row = sb("gm_row", [P, GM_G * GM_D])
        ret_row = sb("ret_row", [P, RH * RV])
        lat_row = gm_row
        ident = sb("ident", [P, P])
        zeros = sb("zeros", [P, P])
        rope_ret = sb("rope_ret", [P, BLOCKS, 2, RQK // 2])
        rope_mla = sb("rope_mla", [P, BLOCKS, 2, ROPE // 2])
        decay = sb("decay", [P, RH, P])
        q_decay = sb("q_decay", [P, RH, P])
        k_decay = sb("k_decay", [P, RH])
        decay_row = decay[:].rearrange("p r k -> p (r k)")
        causal = sb("causal", [P, P])
        iota = sb("iota", [P, TOPK])
        wsT = sb("wsT", [P, GM_G, P])
        bsT = sb("bsT", [P, GM_G])
        keysT = sb("keysT", [P, LAYERS * 2, NKEYS])
        krT = sb("krT", [ROPE, BLOCKS * P])
        sums = sb("sums", [P, 4])
        roots = sb("roots", [P, 4])
        rstd = sb("rstd", [P, 4])
        att_max = sb("att_max", [P, MH])
        att_bias = sb("att_bias", [P, MH])
        att_sum = sb("att_sum", [P, MH])
        att_inv = sb("att_inv", [P, MH])
        kr = sb("kr", [P, ROPE])
        top_v = sb("top_v", [P, 2 * PH, TOPK])
        top_f = sb("top_f", [P, 2 * PH, TOPK])
        logits = sb("logits", [P, PH, TOPK])
        gate_sum = sb("gate_sum", [P, PH])
        gates = sb("gates", [P, 2, PICKS])
        experts = sb("experts", [P, 2, PICKS], U32)
        picked = sb("picked", [P, 2, GROUP], U32)
        dots = sb("dots", [P, GROUP])
        gelus = sb("gelus", [P, GROUP])
        pick_w = sb("pick_w", [P, GROUP])
        diag = sb("diag", [P, DIAGS, P])

        def area(i, n=1):
            return work[:, i:i + n, :].rearrange("p a n -> p (a n)")

        hT = area(0)
        gm_u, gm_v, qk, ret_v, gate, qkT = (area(i) for i in range(1, 7))
        sT, decayed = area(7)[:, 0:512], area(7)[:, 512:1024]
        y = area(8, 2)
        yT = area(10, 2)
        ret_o, junk0 = area(10), area(11)
        state = area(12)
        cn, cT, qr, qrT, qnT = (area(i) for i in range(1, 6))
        att = area(6, 2).rearrange("p (h k) -> p h k", h=MH)
        pT = area(3, 2)
        att_o, oT = area(1), area(2)
        knT = area(9, 2).rearrange("p (h k) -> p h k", h=MH)
        vals = area(11, 2).rearrange("p (b n) -> p b n", b=BLOCKS)
        junk = area(8)
        qry, qryT = area(1, 2), area(3, 2)
        side_u = area(0)[:, 0:256].bitcast(U32).rearrange("p (s k) -> p s k", s=2)
        side_f = area(0)[:, 256:512].rearrange("p (s k) -> p s k", s=2)
        side_e = area(0)[:, 512:768].rearrange("p (s k) -> p s k", s=2)
        top_i = area(0)[:, 768:1024].bitcast(U32).rearrange("p (j k) -> p j k", k=TOPK)
        sc, sc_rest = (t.rearrange("p (j k) -> p j k", k=NKEYS) for t in (area(1, 2), area(3, 2)))
        cand, cand_rest = (t.rearrange("p (j k) -> p j k", k=TOPK * TOPK) for t in (area(5, 2), area(7, 2)))
        best_v = area(1)[:, 0:PICKS].rearrange("p (m k) -> p m k", k=TOPK)
        best_i = area(1)[:, PICKS:2 * PICKS].bitcast(U32).rearrange("p (m k) -> p m k", k=TOPK)
        hot = area(1, 2).rearrange("p (j k) -> p j k", k=TOPK)
        hot_e = area(3, 2).rearrange("p (j k) -> p j k", k=TOPK)

        ring = ctx.enter_context(nc.psum_tensor("ring", [P, RING, BANK], F32))
        moe = ctx.enter_context(nc.psum_tensor("moe", [P, D], F32))

        consts_landed = sem("consts_landed")
        late_landed = sem("late_landed")
        x_landed = sem("x_landed")
        gain_mix_landed = sem("gain_mix_landed")
        gain_ffn_landed = sem("gain_ffn_landed")
        lat_landed = sem("lat_landed")
        w_landed = [sem(f"w_landed{i}") for i in range(W_SLOTS)]
        psum_full = [sem(f"psum_full{i}") for i in range(RING)]
        psum_evac = [sem(f"psum_evac{i}") for i in range(RING)]
        ws_masked = sem("ws_masked")
        zeros_set = sem("zeros_set")
        normed = sem("normed")
        vec_step = sem("vec_step")
        sums_set = sem("sums_set")
        roots_set = sem("roots_set")
        roped = sem("roped")
        v_normed = sem("v_normed")
        decayed_set = sem("decayed_set")
        y_set = sem("y_set")
        c_set = sem("c_set")
        qr_set = sem("qr_set")
        max_set = sem("max_set")
        probs_set = sem("probs_set")
        logits_set = sem("logits_set")
        exp_set = sem("exp_set")
        experts_set = sem("experts_set")
        picked_set = sem("picked_set")
        u_landed = [sem(f"u_landed{i}") for i in range(GROUP)]
        v_landed = [sem(f"v_landed{i}") for i in range(GROUP)]
        gathers_begun = sem("gathers_begun")
        u_free = sem("u_free")
        v_free = sem("v_free")
        dots_set = sem("dots_set")
        gelus_set = sem("gelus_set")
        pick_w_set = sem("pick_w_set")
        diag_set = sem("diag_set")
        moe_full = sem("moe_full")
        moe_added = sem("moe_added")
        final_set = sem("final_set")
        out_landed = sem("out_landed")

        def wait_full(eng, u, name):
            n = PRODUCT[u, name]
            eng.wait_ge(psum_full[n % RING], n // RING + 1)
            return ring[:, n % RING, :]

        def wait_evac(eng, u, *names):
            for name in names:
                n = PRODUCT[u, name]
                eng.wait_ge(psum_evac[n % RING], n // RING + 1)

        def evac_of(u, name):
            return psum_evac[PRODUCT[u, name] % RING]

        def full_of(u, name):
            return psum_full[PRODUCT[u, name] % RING]

        chunks = []

        def rows(w, k0, nk, c0, nc_):
            return w[k0 * P:(k0 + nk) * P, c0:c0 + nc_].rearrange("(k p) n -> p k n", p=P)

        for u in range(UNITS):
            if layer_of(u) == 0:
                for n in IN_ORDER:
                    chunks += [(rows(a["hy_w_in"], k, 4, n * BANK, BANK), u, f"in{n}") for k in (0, 4)]
                for n in range(2):
                    chunks += [(rows(a["hy_w_out"], k, 4, n * BANK, BANK), u, f"out{n}") for k in (0, 4, 8, 12)]
            else:
                chunks += [(rows(a["mla_w_down"], k, 2, 0, DOWN), u, "down1") for k in range(0, KD, 2)]
                chunks += [(rows(a["mla_w_q_up"], k, 1, 0, MH * QKD), u, "qn1") for k in range(QR // P)]
                chunks += [(rows(a["mla_w_kv_up"], k, 1, 0, MH * 2 * NOPE), u, "v1") for k in range(KVR // P)]
                for n in range(2):
                    chunks += [(rows(a["mla_w_out"], k, 4, n * BANK, BANK), u, f"out{n}") for k in (0, 4)]
            for n in range(4):
                chunks += [(rows(a["peer_w_q"][layer_of(u)], k, 4, n * BANK, BANK), u, f"q{n}") for k in (0, 4)]

        def chunk_tile(i):
            src = chunks[i][0]
            nk, n = src.shape[1], src.shape[2]
            return w_ring[:, i % W_SLOTS, 0:nk * n].rearrange("p (k n) -> p k n", k=nk)

        schedule = plan_schedule()
        early = [(ident[:], a["c_ident"]), (rope_ret[:], a["c_rope_ret"]), (decay[:], a["c_decay"]),
                 (k_decay[:], a["c_k_decay"]), (bsT[:], a["gm_b_sT"]),
                 (gm_row[:], a["gm_v_norm"].broadcast_to([P, D])), (wsT[:], a["gm_w_sT"])]
        late = [(ret_row[:], a["ret_norm"].broadcast_to([P, D])), (q_decay[:], a["c_q_decay"]),
                (keysT[:], a["peer_keysT"]), (iota[:], a["c_iota"]), (rope_mla[:], a["c_rope_mla"]),
                (causal[:], a["c_causal"])]

        block = ctx.enter_context(nc.Block())

        @block.sync
        def _(sp):
            sp.dma_start(x[:, 0, :], a["x"][0:P, :]).then_inc(x_landed, 16)
            sp.dma_start(gain_mix[:], a["norm_mix"][0:1, :].broadcast_to([P, D])).then_inc(gain_mix_landed, 16)
            for i, (src, u, name) in enumerate(chunks):
                first = i == 0 or chunks[i - 1][1] != u
                if first and u == BLOCKS:
                    sp.wait_ge(normed, 2 * (BLOCKS - 1) + 1)
                    sp.dma_start(gain_mix[:], a["norm_mix"][1:2, :].broadcast_to([P, D])).then_inc(gain_mix_landed, 16)
                    sp.wait_ge(v_normed, BLOCKS)
                    sp.dma_start(lat_row[:, 0:QR], a["mla_q_norm"].broadcast_to([P, QR])).then_inc(lat_landed, 16)
                    sp.dma_start(lat_row[:, QR:QR + KVR], a["mla_kv_norm"].broadcast_to([P, KVR])).then_inc(lat_landed, 16)
                if i >= W_SLOTS:
                    _, uu, last_user = chunks[i - W_SLOTS]
                    wait_full(sp, uu, last_user)
                sp.dma_start(chunk_tile(i), src).then_inc(w_landed[i % W_SLOTS], 16)
                if i == W_SLOTS - 1:
                    sp.dma_start(gain_ffn[:], a["norm_ffn"][0:1, :].broadcast_to([P, D])).then_inc(gain_ffn_landed, 16)
                    sp.dma_start(x[:, 1, :], a["x"][P:2 * P, :]).then_inc(x_landed, 16)
                if name == "out0" and u == BLOCKS and chunks[i - 1][2] != "out0":
                    sp.wait_ge(normed, 2 * BLOCKS)
                    sp.dma_start(gain_ffn[:], a["norm_ffn"][1:2, :].broadcast_to([P, D])).then_inc(gain_ffn_landed, 16)
            sp.wait_ge(normed, 2 * UNITS - 1)
            sp.dma_start(gain_mix[:], a["final_norm"].broadcast_to([P, D])).then_inc(gain_mix_landed, 16)
            for b in range(BLOCKS):
                sp.wait_ge(final_set, b + 1)
                sp.dma_start(out[b * P:(b + 1) * P, :], h[:, b, :]).then_inc(out_landed, 16)
            sp.wait_ge(out_landed, 16 * BLOCKS)

        @block.gpsimd
        def _(pool):
            pool.wait_ge(consts_landed, 16 * len(early))
            nc.gpsimd.affine_select(out=wsT[:], in_=wsT[:], compare_op=ALU.is_ge, fill=0.0, base=0,
                                    pattern=[[0, GM_G], [1, P]], channel_multiplier=-1).then_inc(ws_masked, 1)

            def gather(u, rows_sb, table, k, half, landed):
                pool.sem_inc(gathers_begun, 1)
                pool.indirect_dma_start(rows_sb[:, k, :], None, table,
                                        bass.IndirectOffsetOnAxis(picked[:, half, k:k + 1], 0)).then_inc(landed[k], 16)

            def picks(u, g0, n):
                assert g0 % 2 == 0 and n % 2 == 0
                pool.wait_ge(experts_set, u + 1)
                base = u * GROUPS + g0
                with nc.gpsimd.Fori(0, n // 2) as i:
                    for half in range(2):
                        group = i * 2 + (base + half)
                        nc.gpsimd.tensor_copy(picked[:, half, :],
                                              experts[:, u % 2, bass.ds(i * 2 * GROUP + (g0 + half) * GROUP, GROUP)]
                                              ).then_inc(picked_set, 1)
                        pool.wait_ge(picked_set, group + 1)
                        for k in range(GROUP):
                            pool.wait_ge(u_free, group * GROUP + (k + 1))
                            gather(u, u_rows, a["peer_u"], k, half, u_landed)
                        for k in range(GROUP):
                            pool.wait_ge(v_free, group * GROUP + (k + 1))
                            gather(u, v_rows, a["peer_v"], k, half, v_landed)

            for step in schedule:
                if step[0] == "picks":
                    picks(*step[1:])

        @block.tensor
        def _(pe):
            at = [0]

            def fill(u, name):
                n = PRODUCT[u, name]
                if n >= RING:
                    pe.wait_ge(psum_evac[n % RING], n // RING)
                return ring[:, n % RING, :]

            def next_chunk():
                i = at[0]
                at[0] += 1
                pe.wait_ge(w_landed[i % W_SLOTS], 16 * (i // W_SLOTS + 1))
                return chunk_tile(i)

            def transposes(u, name, src, count, width=P):
                bank = fill(u, name)
                for j in range(count):
                    last = nc.tensor.transpose(bank[0:width, j * P:(j + 1) * P], src[:, j * width:(j + 1) * width], ident[:])
                last.then_inc(full_of(u, name), 1)

            def project(u, name, actT, steps):
                bank = fill(u, name)
                for k in range(steps):
                    if k % 4 == 0:
                        w = next_chunk()
                    last = nc.tensor.matmul(bank, actT[:, k * P:(k + 1) * P], w[:, k % 4, :],
                                            start=k == 0, stop=k == steps - 1)
                last.then_inc(full_of(u, name), 1)

            def mixer0(u):
                b = block_of(u)
                pe.wait_ge(consts_landed, 16 * len(early))
                pe.wait_ge(normed, 2 * u + 1)
                for i in range(2):
                    transposes(u, f"hT{i}", h[:, u % 2, i * 512:(i + 1) * 512], 4)
                wait_evac(pe, u, "hT0", "hT1")
                for n in IN_ORDER:
                    project(u, f"in{n}", hT, KD)
                pe.wait_ge(roped, 2 * (u + 1))
                for i in range(2):
                    transposes(u, f"qkT{i}", qk[:, i * 512:(i + 1) * 512], RH)
                wait_evac(pe, u, "qkT0", "qkT1")
                bank = fill(u, "ret_s")
                for r in range(RH):
                    last = nc.tensor.matmul(bank[:, r * P:(r + 1) * P], qkT[:, 512 + r * P:512 + (r + 1) * P],
                                            qkT[:, r * P:(r + 1) * P], start=True, stop=True)
                last.then_inc(full_of(u, "ret_s"), 1)
                pe.wait_ge(v_normed, u + 1)
                pe.wait_ge(ws_masked, 1)
                for i in range(2):
                    bank = fill(u, f"mix{i}")
                    for j in range(2):
                        g = 2 * i + j
                        last = nc.tensor.matmul(bank[:, j * GM_D:(j + 1) * GM_D], wsT[:, g, :],
                                                gm_v[:, g * GM_D:(g + 1) * GM_D], start=True, stop=True)
                    last.then_inc(full_of(u, f"mix{i}"), 1)
                wait_evac(pe, u, "in6", "in7", "ret_s")
                pe.wait_ge(decayed_set, u + 1)
                for i in range(2):
                    bank = fill(u, f"ret_o{i}")
                    for j in range(2):
                        r = 2 * i + j
                        part = bank[:, j * RV:(j + 1) * RV]
                        last = nc.tensor.matmul(part, sT[:, r * P:(r + 1) * P], ret_v[:, r * RV:(r + 1) * RV],
                                                start=True, stop=b == 0)
                        if b == 1:
                            last = nc.tensor.matmul(part, decayed[:, r * P:(r + 1) * P], state[:, r * RV:(r + 1) * RV],
                                                    start=False, stop=True)
                    last.then_inc(full_of(u, f"ret_o{i}"), 1)
                if b == 0:
                    for i in range(2):
                        bank = fill(u, f"st{i}")
                        for j in range(2):
                            r = 2 * i + j
                            last = nc.tensor.matmul(bank[:, j * RV:(j + 1) * RV], decayed[:, r * P:(r + 1) * P],
                                                    ret_v[:, r * RV:(r + 1) * RV], start=True, stop=True)
                        last.then_inc(full_of(u, f"st{i}"), 1)
                pe.wait_ge(y_set, u + 1)
                for i in range(4):
                    transposes(u, f"yT{i}", y[:, i * 512:(i + 1) * 512], 4)
                wait_evac(pe, u, "yT0", "yT1", "yT2", "yT3")
                for i in range(2):
                    project(u, f"out{i}", yT, 2 * KD)

            def mixer1(u):
                b = block_of(u)
                keys = (b + 1) * P
                pe.wait_ge(normed, 2 * u + 1)
                for i in range(2):
                    transposes(u, f"hT{i}", h[:, u % 2, i * 512:(i + 1) * 512], 4)
                wait_evac(pe, u, "hT0", "hT1")
                down0, down1 = fill(u, "down0"), fill(u, "down1")
                for k in range(KD):
                    if k % 2 == 0:
                        w = next_chunk()
                    first = nc.tensor.matmul(down0[:, 0:QR], hT[:, k * P:(k + 1) * P], w[:, k % 2, 0:QR],
                                             start=k == 0, stop=k == KD - 1)
                    last = nc.tensor.matmul(down1[:, 0:DOWN - QR], hT[:, k * P:(k + 1) * P], w[:, k % 2, QR:DOWN],
                                            start=k == 0, stop=k == KD - 1)
                first.then_inc(full_of(u, "down0"), 1)
                last.then_inc(full_of(u, "down1"), 1)
                pe.wait_ge(c_set, (u - BLOCKS) + 1)
                transposes(u, "cT0", cn, QR // P)
                transposes(u, "cT1", cn[:, QR:QR + KVR], KVR // P)
                transposes(u, "krT", kr[:], 1, ROPE)
                wait_evac(pe, u, "cT0", "cT1")
                wq = [next_chunk()[:, 0, :] for _ in range(QR // P)]
                heads = [w.rearrange("p (m n) -> p m n", m=MH) for w in wq]
                bank = fill(u, "qr")
                for k in range(QR // P):
                    last = nc.tensor.matmul(bank, cT[:, k * P:(k + 1) * P], heads[k][:, :, NOPE:QKD],
                                            start=k == 0, stop=k == QR // P - 1)
                last.then_inc(full_of(u, "qr"), 1)
                for i in range(2):
                    bank = fill(u, f"qn{i}")
                    for j in range(4):
                        for k in range(QR // P):
                            last = nc.tensor.matmul(bank[:, j * P:(j + 1) * P], heads[k][:, 4 * i + j, 0:NOPE],
                                                    cT[:, k * P:(k + 1) * P], start=k == 0, stop=k == QR // P - 1)
                    last.then_inc(full_of(u, f"qn{i}"), 1)
                kvT = cT[:, QR:QR + KVR]
                wkv = [next_chunk()[:, 0, :].rearrange("p (m n) -> p m n", m=MH) for _ in range(KVR // P)]
                for i in range(2):
                    bank = fill(u, f"kn{i}")
                    for j in range(4):
                        for k in range(KVR // P):
                            last = nc.tensor.matmul(bank[:, j * P:(j + 1) * P], wkv[k][:, 4 * i + j, 0:NOPE],
                                                    kvT[:, k * P:(k + 1) * P], start=k == 0, stop=k == KVR // P - 1)
                    last.then_inc(full_of(u, f"kn{i}"), 1)
                for i in range(2):
                    bank = fill(u, f"v{i}")
                    for k in range(KVR // P):
                        last = nc.tensor.matmul(bank, kvT[:, k * P:(k + 1) * P], wkv[k][:, 4 * i:4 * i + 4, NOPE:2 * NOPE],
                                                start=k == 0, stop=k == KVR // P - 1)
                    last.then_inc(full_of(u, f"v{i}"), 1)
                pe.wait_ge(qr_set, (u - BLOCKS) + 1)
                for i in range(2):
                    transposes(u, f"qrT{i}", qr[:, i * 4 * ROPE:(i + 1) * 4 * ROPE], 4, ROPE)
                wait_evac(pe, u, "krT", "qn0", "qn1", "kn0", "kn1", "qrT0", "qrT1")
                per = BANK // keys
                for i in range(MH // per):
                    bank = fill(u, f"s{i}")
                    for j in range(per):
                        m = i * per + j
                        part = bank[:, j * keys:(j + 1) * keys]
                        nc.tensor.matmul(part, qnT[:, m * P:(m + 1) * P], knT[:, m, 0:keys], start=True, stop=False)
                        last = nc.tensor.matmul(part, qrT[0:ROPE, m * P:(m + 1) * P], krT[:, 0:keys], start=False, stop=True)
                    last.then_inc(full_of(u, f"s{i}"), 1)
                pe.wait_ge(probs_set, (u - BLOCKS) + 1)
                for i in range(2 * (b + 1)):
                    bank = fill(u, f"pT{i}")
                    for j in range(4):
                        m, kb = divmod(4 * i + j, b + 1)
                        last = nc.tensor.transpose(bank[:, j * P:(j + 1) * P], att[:, m, kb * P:(kb + 1) * P], ident[:])
                    last.then_inc(full_of(u, f"pT{i}"), 1)
                wait_evac(pe, u, "v0", "v1", *[f"pT{i}" for i in range(2 * (b + 1))])
                for i in range(2):
                    bank = fill(u, f"o{i}")
                    for j in range(4):
                        m = 4 * i + j
                        for kb in range(b + 1):
                            n = m * (b + 1) + kb
                            last = nc.tensor.matmul(bank[:, j * P:(j + 1) * P], pT[:, n * P:(n + 1) * P],
                                                    vals[:, kb, m * MV:(m + 1) * MV], start=kb == 0, stop=kb == b)
                    last.then_inc(full_of(u, f"o{i}"), 1)
                wait_evac(pe, u, "o0", "o1")
                for i in range(2):
                    transposes(u, f"oT{i}", att_o[:, i * 512:(i + 1) * 512], 4)
                wait_evac(pe, u, "oT0", "oT1")
                for i in range(2):
                    project(u, f"out{i}", oT, KD)

            def route(u):
                if u == 0:
                    pe.wait_ge(late_landed, 16 * len(late))
                pe.wait_ge(normed, 2 * u + 2)
                for i in range(2):
                    transposes(u, f"fT{i}", h[:, u % 2, i * 512:(i + 1) * 512], 4)
                wait_evac(pe, u, "fT0", "fT1")
                for i in range(4):
                    project(u, f"q{i}", hT, KD)
                for i in range(4):
                    wait_evac(pe, u, f"q{i}")
                    transposes(u, f"qT{i}", qry[:, i * 512:(i + 1) * 512], 4)
                for i in range(4):
                    wait_evac(pe, u, f"qT{i}")
                    bank = fill(u, f"sc{i}")
                    for j in range(4):
                        n = 4 * i + j
                        last = nc.tensor.matmul(bank[:, j * P:(j + 1) * P], qryT[:, n * P:(n + 1) * P],
                                                keysT[:, layer_of(u) * 2 + n % 2, :], start=True, stop=True)
                    last.then_inc(full_of(u, f"sc{i}"), 1)

            def picks(u, g0, n):
                if g0 == 0:
                    pe.wait_ge(zeros_set, 1)
                    if u:
                        pe.wait_ge(moe_added, u)
                    for c in range(2):
                        nc.tensor.matmul(moe[:, c * BANK:(c + 1) * BANK], zeros[:], decay_row,
                                         start=True, stop=False, skip_group_check=True)
                base = u * GROUPS + g0
                with nc.tensor.Fori(0, n) as i:
                    group = i + base
                    for k in range(GROUP):
                        pe.wait_ge(diag_set, group * GROUP + (k + 1))
                        pe.wait_ge(v_landed[k], group * 16 + 16)
                        for c in range(2):
                            last = nc.tensor.matmul(moe[:, c * BANK:(c + 1) * BANK], diag[:, k % DIAGS, :],
                                                    v_rows[:, k, c * BANK:(c + 1) * BANK],
                                                    start=False, stop=False, skip_group_check=True)
                        last.then_inc(v_free, 1)
                if g0 + n == GROUPS:
                    for c in range(2):
                        last = nc.tensor.matmul(moe[:, c * BANK:(c + 1) * BANK], zeros[:], decay_row,
                                                start=False, stop=True, skip_group_check=True)
                    last.then_inc(moe_full, 1)

            for step in schedule:
                if step[0] == "mixer":
                    (mixer1 if layer_of(step[1]) else mixer0)(step[1])
                elif step[0] == "route":
                    route(step[1])
                elif step[0] == "picks":
                    picks(*step[1:])

        @block.scalar
        def _(act):
            for dst, src in early:
                act.dma_start(dst, src).then_inc(consts_landed, 16)
            for dst, src in late:
                act.dma_start(dst, src).then_inc(late_landed, 16)

            def evacuate(u, name, dst, func=ACT.Copy, width=BANK, parts=P):
                bank = wait_full(act, u, name)
                nc.scalar.activation(dst, bank[0:parts, 0:width], func).then_inc(evac_of(u, name), 1)

            norms = [0]

            def take_roots(n):
                norms[0] += 1
                act.wait_ge(sums_set, norms[0])
                nc.scalar.activation(roots[:, 0:n], sums[:, 0:n], ACT.Sqrt).then_inc(roots_set, 1)

            def half(t, i, n=BANK):
                return t[:, i * n:(i + 1) * n]

            def mixer0(u):
                take_roots(1)
                for i in range(2):
                    evacuate(u, f"hT{i}", half(hT, i))
                for i in range(2):
                    evacuate(u, f"in{2 + i}", half(gm_v, i), ACT.Gelu)
                for i in range(2):
                    evacuate(u, f"in{i}", half(gm_u, i), ACT.Gelu)
                take_roots(GM_G)
                for i in range(2):
                    evacuate(u, f"in{6 + i}", half(ret_v, i))
                for i in range(2):
                    evacuate(u, f"in{8 + i}", half(gate, i), ACT.Silu)
                for i in range(2):
                    evacuate(u, f"qkT{i}", half(qkT, i))
                for i in range(2):
                    evacuate(u, f"ret_o{i}", half(ret_o, i))
                take_roots(RH)
                if block_of(u) == 0:
                    for i in range(2):
                        evacuate(u, f"st{i}", half(state, i))
                for i in range(4):
                    evacuate(u, f"yT{i}", half(yT, i))

            def mixer1(u):
                b = block_of(u)
                take_roots(1)
                for i in range(2):
                    evacuate(u, f"hT{i}", half(hT, i))
                evacuate(u, "down0", cn[:, 0:QR], width=QR)
                evacuate(u, "down1", cn[:, QR:DOWN], width=DOWN - QR)
                take_roots(2)
                evacuate(u, "cT0", cT[:, 0:QR], width=QR)
                evacuate(u, "cT1", cT[:, QR:QR + KVR], width=KVR)
                evacuate(u, "krT", krT[:, b * P:(b + 1) * P], width=P, parts=ROPE)
                for i in range(2):
                    evacuate(u, f"qn{i}", half(qnT, i))
                for i in range(2):
                    bank = wait_full(act, u, f"kn{i}")
                    nc.scalar.activation(knT[:, 4 * i:4 * i + 4, b * P:(b + 1) * P],
                                         bank.rearrange("p (m k) -> p m k", m=4), ACT.Copy).then_inc(evac_of(u, f"kn{i}"), 1)
                for i in range(2):
                    evacuate(u, f"v{i}", vals[:, b, i * BANK:(i + 1) * BANK])
                for i in range(2):
                    evacuate(u, f"qrT{i}", qrT[0:ROPE, i * BANK:(i + 1) * BANK], parts=ROPE)
                act.wait_ge(max_set, (u - BLOCKS) + 1)
                for m in range(MH):
                    part = att[:, m, 0:(b + 1) * P]
                    last = nc.scalar.activation(part, part, ACT.Exp, bias=att_bias[:, m:m + 1], scale=ATT_SCALE,
                                                accum_out=att_sum[:, m:m + 1])
                last.then_inc(probs_set, 1)
                for i in range(2 * (b + 1)):
                    evacuate(u, f"pT{i}", half(pT, i))
                for i in range(2):
                    evacuate(u, f"oT{i}", half(oT, i))

            def route(u):
                take_roots(1)
                for i in range(2):
                    evacuate(u, f"fT{i}", half(hT, i))
                for i in range(4):
                    evacuate(u, f"q{i}", half(qry, i))
                for i in range(4):
                    evacuate(u, f"qT{i}", half(qryT, i))
                for i in range(4):
                    evacuate(u, f"sc{i}", half(area(1, 2), i))
                act.wait_ge(logits_set, u + 1)
                nc.scalar.activation(logits[:], logits[:], ACT.Exp).then_inc(exp_set, 1)

            def picks(u, g0, n):
                base = u * GROUPS + g0
                with nc.scalar.Fori(0, n) as i:
                    group = i + base
                    act.wait_ge(dots_set, group + 1)
                    nc.scalar.activation(gelus[:], dots[:], ACT.Gelu).then_inc(gelus_set, 1)
                    act.wait_ge(pick_w_set, group + 1)
                    for k in range(GROUP):
                        act.wait_ge(v_free, group * GROUP + (k + 1 + GROUP - DIAGS))
                        nc.scalar.mul(diag[:, k % DIAGS, :], ident[:], pick_w[:, k:k + 1]).then_inc(diag_set, 1)

            for step in schedule:
                if step[0] == "mixer":
                    (mixer1 if layer_of(step[1]) else mixer0)(step[1])
                elif step[0] == "route":
                    route(step[1])
                elif step[0] == "picks":
                    picks(*step[1:])
                else:
                    take_roots(1)

        @block.vector
        def _(dve):
            steps, norms = [0], [0]

            def step_done(ins):
                ins.then_inc(vec_step, 1)
                steps[0] += 1
                dve.wait_ge(vec_step, steps[0])

            nc.vector.memset(zeros[:], 0.0).then_inc(zeros_set, 1)

            def inverse_rms(parts, scratch):
                at = 0
                for i, part in enumerate(parts):
                    width = part.shape[1]
                    last = nc.vector.tensor_tensor_reduce(out=scratch[:, at:at + width], in0=part, in1=part, scale=1.0 / width,
                                                          scalar=EPS, op0=ALU.mult, op1=ALU.add, accum_out=sums[:, i:i + 1])
                    at += width
                last.then_inc(sums_set, 1)
                norms[0] += 1
                dve.wait_ge(roots_set, norms[0])
                step_done(nc.vector.reciprocal(rstd[:, 0:len(parts)], roots[:, 0:len(parts)]))

            def norm_tokens(src, gain, dst, scratch):
                inverse_rms([src], scratch)
                return nc.vector.scalar_tensor_tensor(out=dst, in0=src, scalar=rstd[:, 0:1], in1=gain,
                                                      op0=ALU.mult, op1=ALU.mult)

            def add_output(u):
                for i in range(2):
                    bank = wait_full(dve, u, f"out{i}")
                    part = x[:, block_of(u), i * BANK:(i + 1) * BANK]
                    nc.vector.tensor_tensor(part, bank, part, ALU.add).then_inc(evac_of(u, f"out{i}"), 1)
                wait_evac(dve, u, "out0", "out1")

            def rotate(u, name, dst, table, heads, half, scratch, src=None):
                bank = (wait_full(dve, u, name) if src is None else src)
                width = heads * 2 * half
                v = bank[:, 0:width].rearrange("p (n k) -> p n k", k=half)
                cos = table[:, 0, :].unsqueeze(1).broadcast_to([P, 2 * heads, half])
                sin = table[:, 1, :].unsqueeze(1).broadcast_to([P, 2 * heads, half])
                d = dst[:, 0:width].rearrange("p (n k) -> p n k", k=half)
                t = scratch[:, 0:width].rearrange("p (n k) -> p n k", k=half)
                by_cos = nc.vector.tensor_tensor(d, v, cos, ALU.mult)
                by_sin = nc.vector.tensor_tensor(t, v, sin, ALU.mult)
                if src is None:
                    by_sin.then_inc(evac_of(u, name), 1)
                    wait_evac(dve, u, name)
                else:
                    step_done(by_sin)
                d4 = dst[:, 0:width].rearrange("p (n s k) -> p n s k", s=2, k=half)
                t4 = scratch[:, 0:width].rearrange("p (n s k) -> p n s k", s=2, k=half)
                nc.vector.tensor_tensor(d4[:, :, 0, :], d4[:, :, 0, :], t4[:, :, 1, :], ALU.subtract)
                return nc.vector.tensor_tensor(d4[:, :, 1, :], d4[:, :, 1, :], t4[:, :, 0, :], ALU.add)

            def mixer0(u):
                b = block_of(u)
                if b == 0:
                    dve.wait_ge(x_landed, 16)
                    dve.wait_ge(gain_mix_landed, 16)
                else:
                    dve.wait_ge(x_landed, 32)
                norm_tokens(x[:, b, :], gain_mix[:], h[:, u % 2, :], junk).then_inc(normed, 1)
                if u == 0:
                    dve.wait_ge(consts_landed, 16 * len(early))
                rotate(u, "in4", qk[:, 0:512], rope_ret[:, b], RH, RQK // 2, junk0).then_inc(roped, 1)
                dve.wait_ge(roped, 2 * u + 1)
                rotate(u, "in5", qk[:, 512:1024], rope_ret[:, b], RH, RQK // 2, junk0).then_inc(roped, 1)
                dve.wait_ge(roped, 2 * u + 2)
                if b == 0:
                    nc.vector.tensor_tensor(decayed.rearrange("p (r k) -> p r k", r=RH),
                                            qk[:, 512:1024].rearrange("p (r k) -> p r k", r=RH),
                                            k_decay[:].unsqueeze(2).broadcast_to([P, RH, P]), ALU.mult
                                            ).then_inc(decayed_set, 1)
                wait_evac(dve, u, "in2", "in3")
                inverse_rms([gm_v[:, g * GM_D:(g + 1) * GM_D] for g in range(GM_G)], junk0)
                for g in range(GM_G):
                    part = gm_v[:, g * GM_D:(g + 1) * GM_D]
                    last = nc.vector.scalar_tensor_tensor(out=part, in0=part, scalar=rstd[:, g:g + 1],
                                                          in1=gm_row[:, g * GM_D:(g + 1) * GM_D], op0=ALU.mult, op1=ALU.mult)
                last.then_inc(v_normed, 1)
                wait_evac(dve, u, "in8", "in9")
                if u == 0:
                    dve.wait_ge(late_landed, 16 * len(late))
                step_done(nc.vector.tensor_tensor(gate, gate, ret_row[:], ALU.mult))
                if b == 1:
                    wait_evac(dve, u, "qkT0")
                    nc.vector.tensor_tensor(decayed.rearrange("p (r k) -> p r k", r=RH),
                                            qkT[:, 0:512].rearrange("p (r k) -> p r k", r=RH), q_decay[:], ALU.mult
                                            ).then_inc(decayed_set, 1)
                bank = wait_full(dve, u, "ret_s")
                nc.vector.tensor_tensor(sT.rearrange("p (r k) -> p r k", r=RH), bank.rearrange("p (r k) -> p r k", r=RH),
                                        decay[:], ALU.mult).then_inc(evac_of(u, "ret_s"), 1)
                wait_evac(dve, u, "in0", "in1")
                for i in range(2):
                    bank = wait_full(dve, u, f"mix{i}")
                    for j in range(2):
                        g = 2 * i + j
                        last = nc.vector.scalar_tensor_tensor(out=y[:, g * GM_D:(g + 1) * GM_D], in0=bank[:, j * GM_D:(j + 1) * GM_D],
                                                              scalar=bsT[:, g:g + 1], in1=gm_u[:, g * GM_D:(g + 1) * GM_D],
                                                              op0=ALU.add, op1=ALU.mult)
                    last.then_inc(evac_of(u, f"mix{i}"), 1)
                wait_evac(dve, u, "ret_o0", "ret_o1")
                inverse_rms([ret_o[:, r * RV:(r + 1) * RV] for r in range(RH)], junk0)
                for r in range(RH):
                    last = nc.vector.scalar_tensor_tensor(out=y[:, 1024 + r * RV:1024 + (r + 1) * RV], in0=ret_o[:, r * RV:(r + 1) * RV],
                                                          scalar=rstd[:, r:r + 1], in1=gate[:, r * RV:(r + 1) * RV],
                                                          op0=ALU.mult, op1=ALU.mult)
                last.then_inc(y_set, 1)
                add_output(u)

            def mixer1(u):
                b = block_of(u)
                keys = (b + 1) * P
                dve.wait_ge(gain_mix_landed, 32)
                norm_tokens(x[:, b, :], gain_mix[:], h[:, u % 2, :], junk).then_inc(normed, 1)
                wait_evac(dve, u, "down0", "down1")
                dve.wait_ge(lat_landed, 32)
                inverse_rms([cn[:, 0:QR], cn[:, QR:QR + KVR]], junk)
                for i, (lo, hi) in enumerate(((0, QR), (QR, QR + KVR))):
                    nc.vector.scalar_tensor_tensor(out=cn[:, lo:hi], in0=cn[:, lo:hi], scalar=rstd[:, i:i + 1],
                                                   in1=lat_row[:, lo:hi], op0=ALU.mult, op1=ALU.mult)
                rotate(u, None, kr[:], rope_mla[:, b], 1, ROPE // 2, junk, src=cn[:, QR + KVR:DOWN]).then_inc(c_set, 1)
                rotate(u, "qr", qr[:, 0:512], rope_mla[:, b], MH, ROPE // 2, junk).then_inc(qr_set, 1)
                per = BANK // keys
                for i in range(MH // per):
                    bank = wait_full(dve, u, f"s{i}").rearrange("p (m k) -> p m k", k=keys)
                    rows_of = att[:, i * per:(i + 1) * per, :]
                    if b:
                        nc.vector.tensor_copy(rows_of[:, :, 0:P], bank[:, :, 0:P])
                    nc.vector.tensor_tensor(rows_of[:, :, b * P:keys], bank[:, :, b * P:keys],
                                            causal[:].unsqueeze(1).broadcast_to([P, per, P]), ALU.add
                                            ).then_inc(evac_of(u, f"s{i}"), 1)
                wait_evac(dve, u, *[f"s{i}" for i in range(MH // per)])
                step_done(nc.vector.tensor_reduce(att_max[:], att[:, :, 0:keys], AX, ALU.max))
                nc.vector.tensor_scalar(att_bias[:], att_max[:], -ATT_SCALE, None, ALU.mult).then_inc(max_set, 1)
                dve.wait_ge(probs_set, (u - BLOCKS) + 1)
                step_done(nc.vector.reciprocal(att_inv[:], att_sum[:]))
                for i in range(2):
                    bank = wait_full(dve, u, f"o{i}")
                    nc.vector.tensor_tensor(att_o[:, i * BANK:(i + 1) * BANK].rearrange("p (m k) -> p m k", m=4),
                                            bank.rearrange("p (m k) -> p m k", m=4),
                                            att_inv[:, 4 * i:4 * i + 4].unsqueeze(2).broadcast_to([P, 4, MV]), ALU.mult
                                            ).then_inc(evac_of(u, f"o{i}"), 1)
                add_output(u)

            def best16(n, values, rest, out_v, out_i):
                for j in range(n):
                    last = nc.vector.max(out_v[:, j, 0:8], values[:, j, :])
                step_done(last)
                for j in range(n):
                    nc.vector.max_index(out_i[:, j, 0:8], out_v[:, j, 0:8], values[:, j, :])
                for j in range(n):
                    last = nc.vector.match_replace(rest[:, j, :], out_v[:, j, 0:8], values[:, j, :], LOWEST)
                step_done(last)
                for j in range(n):
                    last = nc.vector.max(out_v[:, j, 8:16], rest[:, j, :])
                step_done(last)
                for j in range(n):
                    last = nc.vector.max_index(out_i[:, j, 8:16], out_v[:, j, 8:16], rest[:, j, :])
                step_done(last)

            def route(u):
                b, lay, par = block_of(u), layer_of(u), u % 2
                dve.wait_ge(gain_ffn_landed, 16 * (lay + 1))
                norm_tokens(x[:, b, :], gain_ffn[:], h[:, par, :], junk).then_inc(normed, 1)
                wait_evac(dve, u, "sc0", "sc1", "sc2", "sc3")
                best16(2 * PH, sc, sc_rest, top_v, top_i)
                step_done(nc.vector.tensor_copy(top_f[:], top_i))
                pair = top_v[:].rearrange("p (m s) k -> p m s k", s=2)
                step_done(nc.vector.tensor_tensor(cand.rearrange("p m (i j) -> p m i j", i=TOPK),
                                                  pair[:, :, 0, :].unsqueeze(3).broadcast_to([P, PH, TOPK, TOPK]),
                                                  pair[:, :, 1, :].unsqueeze(2).broadcast_to([P, PH, TOPK, TOPK]), ALU.add))
                best16(PH, cand, cand_rest, best_v, best_i)
                nc.vector.tensor_tensor(logits[:], best_v, best_v[:, :, 0:1].broadcast_to([P, PH, TOPK]), ALU.subtract
                                        ).then_inc(logits_set, 1)
                flat = best_i.rearrange("p m k -> p (m k)")
                nc.vector.tensor_scalar(side_u[:, 0, :], flat, 4, None, ALU.logical_shift_right)
                step_done(nc.vector.tensor_scalar(side_u[:, 1, :], flat, TOPK - 1, None, ALU.bitwise_and))
                step_done(nc.vector.tensor_copy(side_f, side_u))
                keys = top_f[:].rearrange("p (m s) k -> p m s k", s=2)
                for s in range(2):
                    step_done(nc.vector.tensor_tensor(hot, side_f[:, s, :].unsqueeze(2).broadcast_to([P, PICKS, TOPK]),
                                                      iota[:].unsqueeze(1).broadcast_to([P, PICKS, TOPK]), ALU.is_equal))
                    step_done(nc.vector.tensor_tensor(hot_e.rearrange("p (m k) j -> p m k j", m=PH),
                                                      hot.rearrange("p (m k) j -> p m k j", m=PH),
                                                      keys[:, :, s, :].unsqueeze(2).broadcast_to([P, PH, TOPK, TOPK]), ALU.mult))
                    step_done(nc.vector.tensor_reduce(side_e[:, s, :], hot_e, AX, ALU.add))
                step_done(nc.vector.scalar_tensor_tensor(out=side_f[:, 0, :], in0=side_e[:, 0, :], scalar=float(NKEYS),
                                                         in1=side_e[:, 1, :], op0=ALU.mult, op1=ALU.add))
                nc.vector.tensor_scalar(experts[:, par, :], side_f[:, 0, :], float(lay * N_EXPERTS), None, ALU.add
                                        ).then_inc(experts_set, 1)
                dve.wait_ge(exp_set, u + 1)
                step_done(nc.vector.tensor_reduce(gate_sum[:], logits[:], AX, ALU.add))
                step_done(nc.vector.reciprocal(gate_sum[:], gate_sum[:]))
                step_done(nc.vector.tensor_tensor(gates[:, par, :].rearrange("p (m k) -> p m k", m=PH), logits[:],
                                                  gate_sum[:].unsqueeze(2).broadcast_to([P, PH, TOPK]), ALU.mult))

            nc.vector.memset(dots[:, 0:1], 0.0).then_inc(u_free, GROUP)
            nc.vector.memset(dots[:, 1:2], 0.0).then_inc(v_free, GROUP)

            def picks(u, g0, n):
                base = u * GROUPS + g0
                with nc.vector.Fori(0, n) as i:
                    group = i + base
                    for k in range(GROUP):
                        dve.wait_ge(u_landed[k], group * 16 + 16)
                        last = nc.vector.tensor_tensor_reduce(out=u_rows[:, k, :], in0=u_rows[:, k, :], in1=h[:, u % 2, :],
                                                              scale=1.0, scalar=0.0, op0=ALU.mult, op1=ALU.add,
                                                              accum_out=dots[:, k:k + 1])
                        last.then_inc(u_free, 1)
                    dve.wait_ge(u_free, group * GROUP + 2 * GROUP)
                    nc.vector.tensor_copy(dots[:, 0:1], dots[:, 0:1]).then_inc(dots_set, 1)
                    dve.wait_ge(gelus_set, group + 1)
                    nc.vector.tensor_tensor(pick_w[:], gelus[:], gates[:, u % 2, bass.ds(i * GROUP + g0 * GROUP, GROUP)],
                                            ALU.mult).then_inc(pick_w_set, 1)
                if g0 + n == GROUPS:
                    dve.wait_ge(moe_full, u + 1)
                    part = x[:, block_of(u), :]
                    nc.vector.tensor_tensor(part, moe[:], part, ALU.add).then_inc(moe_added, 1)
                    dve.wait_ge(moe_added, u + 1)

            def final(b):
                dve.wait_ge(gain_mix_landed, 48)
                norm_tokens(x[:, b, :], gain_mix[:], h[:, b, :], junk).then_inc(final_set, 1)

            for step in schedule:
                if step[0] == "mixer":
                    (mixer1 if layer_of(step[1]) else mixer0)(step[1])
                elif step[0] == "route":
                    route(step[1])
                elif step[0] == "picks":
                    picks(*step[1:])
                else:
                    final(step[1])


def shape_constants():
    f = np.float32
    pos = np.arange(P, dtype=f)
    log_gamma = np.log(f(1.0) - f(2.0) ** (f(-5.0) - np.arange(RH, dtype=f))).astype(f)
    diff = pos[:, None] - pos[None, :]
    scale = f(RQK ** -0.5)
    decay = np.where(diff[None] >= 0, np.exp(diff[None] * log_gamma[:, None, None]), f(0.0)).astype(f) * scale
    q_decay = np.exp((pos[:, None] + f(1.0)) * log_gamma[None, :]).astype(f)
    k_decay = np.exp((f(P) - f(1.0) - pos[:, None]) * log_gamma[None, :]).astype(f) * scale

    def rope(half):
        inv = (f(1.0) / (f(10000.0) ** (np.arange(half, dtype=f) / f(half)))).astype(f)
        ang = np.arange(BLOCKS * P, dtype=f)[:, None] * inv[None, :]
        table = np.stack([np.cos(ang), np.sin(ang)], axis=1).astype(f)
        return np.ascontiguousarray(table.reshape(BLOCKS, P, 2, half).transpose(1, 0, 2, 3))

    return {
        "c_ident": np.eye(P, dtype=f),
        "c_rope_ret": rope(RQK // 2),
        "c_rope_mla": rope(ROPE // 2),
        "c_decay": np.ascontiguousarray(decay.transpose(2, 0, 1)),
        "c_q_decay": np.ascontiguousarray(np.broadcast_to(q_decay.T[None], (P, RH, P))),
        "c_k_decay": k_decay,
        "c_causal": np.where(diff >= 0, f(0.0), f(MASKED)).astype(f),
        "c_iota": np.ascontiguousarray(np.broadcast_to(np.arange(TOPK, dtype=f)[None], (P, TOPK))),
    }


def kernel(x, norm_mix, norm_ffn, hy_w_in, gm_v_norm, gm_w_s, gm_b_s, ret_norm, hy_w_out,
           mla_w_down, mla_q_norm, mla_w_q_up, mla_kv_norm, mla_w_kv_up, mla_w_out,
           peer_w_q, peer_sub_keys, peer_u, peer_v, final_norm):
    import concourse.bacc as bacc
    from concourse.bass_utils import run_bass_kernel_spmd as run

    c = np.ascontiguousarray
    arrays = {
        "x": c(x).reshape(BLOCKS * P, D), "norm_mix": c(norm_mix), "norm_ffn": c(norm_ffn),
        "hy_w_in": c(hy_w_in)[0], "gm_v_norm": c(gm_v_norm), "ret_norm": c(ret_norm), "hy_w_out": c(hy_w_out)[0],
        "gm_w_sT": c(np.transpose(c(gm_w_s)[0], (2, 0, 1))), "gm_b_sT": c(np.transpose(c(gm_b_s)[0])),
        "mla_w_down": c(mla_w_down)[0], "mla_q_norm": c(mla_q_norm), "mla_w_q_up": c(mla_w_q_up)[0],
        "mla_kv_norm": c(mla_kv_norm), "mla_w_kv_up": c(mla_w_kv_up)[0], "mla_w_out": c(mla_w_out)[0],
        "peer_w_q": c(peer_w_q),
        "peer_keysT": c(np.transpose(c(peer_sub_keys).reshape(LAYERS * 2, NKEYS, P), (2, 0, 1))),
        "peer_u": c(peer_u).reshape(LAYERS * N_EXPERTS, D), "peer_v": c(peer_v).reshape(LAYERS * N_EXPERTS, D),
        "final_norm": c(final_norm).reshape(1, D),
    }
    arrays.update(shape_constants())
    nc = bacc.Bacc("TRN2", target_bir_lowering=False, num_devices=1)
    a = {n: nc.dram_tensor("in_" + n, v.shape, F32, kind="ExternalInput").ap() for n, v in arrays.items()}
    out = nc.dram_tensor("out_dram", (BLOCKS * P, D), F32, kind="ExternalOutput").ap()
    build(nc, a, out)
    result = run(nc, [{"in_" + n: v for n, v in arrays.items()}], core_ids=[0])
    return result.results[0]["out_dram"].reshape(1, BLOCKS * P, D)
```

```python
from contextlib import ExitStack

import numpy as np

import concourse.bass as bass
from concourse import mybir

ALU = mybir.AluOpType
ACT = mybir.ActivationFunctionType
F32 = mybir.dt.float32
U32 = mybir.dt.uint32
AX = mybir.AxisListType.X

P = 128
D = 1024
KD = D // P
LAYERS, BLOCKS = 2, 2
UNITS = LAYERS * BLOCKS
BANK = 512
EPS = 1e-6

GM_G, GM_D = 4, 256
RH, RQK, RV = 4, 128, 256
QR, KVR = 384, 256
MH, NOPE, ROPE, MV = 8, 128, 64, 128
QKD = NOPE + ROPE
DOWN = QR + KVR + ROPE
ATT_SCALE = QKD ** -0.5
PH, TOPK, NKEYS = 8, 16, 128
N_EXPERTS = NKEYS * NKEYS
PICKS = PH * TOPK

QUARTERS = 4
QH = PH // QUARTERS
QP = PICKS // QUARTERS
GROUP = 8
GROUPS = PICKS // GROUP
TE_PICKS = 5
VE_PICKS = GROUP - TE_PICKS
DIAGS = TE_PICKS
ALL = 2 * GROUPS
RING = 6
W_SLOTS, W_SIZE = 5, 2048
LOWEST = -3.0e38
MASKED = -1.0e30

IN_ORDER = [4, 5, 6, 7, 8, 9, 2, 3, 0, 1]


def layer_of(u):
    return u // BLOCKS


def block_of(u):
    return u % BLOCKS


def plan_products():
    order = []
    for u in range(UNITS):
        if layer_of(u) == 0:
            names = ["hT0", "hT1", "in4", "in5", "in6", "in7", "qkT0", "qkT1", "in8", "in9", "ret_s",
                     "in2", "in3", "ret_o0", "ret_o1"]
            if block_of(u) == 0:
                names += ["st0", "st1"]
            names += ["in0", "in1", "mix0", "mix1", "yT0", "yT1", "yT2", "yT3", "out0", "out1"]
        else:
            n = 2 * (block_of(u) + 1)
            names = ["hT0", "hT1", "down0", "down1", "cT0", "cT1", "krT", "qr", "qn0", "qn1", "kn0", "kn1",
                     "v0", "v1", "qrT0", "qrT1"]
            names += [f"s{i}" for i in range(n)] + [f"pT{i}" for i in range(n)]
            names += ["o0", "o1", "oT0", "oT1", "out0", "out1"]
        names += ["fT0", "fT1"] + [f"{n}{i}" for i in range(QUARTERS) for n in ("q", "qT", "sc")]
        order += [(u, n) for n in names]
    return {key: i for i, key in enumerate(order)}


PRODUCT = plan_products()


class Stages:

    def __init__(self, stages):
        self.stages = stages
        self.after = next(stages, None)

    def run(self, g):
        while self.after is not None and self.after <= g:
            self.after = next(self.stages, None)


def interleave(eng, stages_of, rest_of, begin, group_of_picks, end):
    Stages(stages_of(0)).run(ALL)
    for u in range(UNITS):
        after = Stages(stages_of(u + 1))
        after.run(-1)
        begin(u)
        rest = Stages(rest_of(u) if u == 0 else iter(()))
        group_of_picks(u, 0, True)
        rest.run(0)
        after.run(0)
        g = 1
        while g < GROUPS and (after.after is not None or rest.after is not None):
            group_of_picks(u, g, False)
            rest.run(g)
            after.run(g)
            g += 1
        if GROUPS - g == 1:
            group_of_picks(u, g, False)
        elif g < GROUPS:
            with eng.Fori(g, GROUPS) as i:
                group_of_picks(u, i, False)
        after.run(ALL)
        end(u)
    for _ in stages_of(UNITS + 1):
        pass


def build(nc, a, out):
    with ExitStack() as ctx:
        def sb(name, shape, dt=F32):
            return ctx.enter_context(nc.sbuf_tensor(name, shape, dt))

        def sem(name):
            return ctx.enter_context(nc.semaphore(name))

        x = sb("x", [P, BLOCKS, D])
        h = sb("h", [P, 2, D])
        w_ring = sb("w_ring", [P, W_SLOTS, W_SIZE])
        u_rows = sb("u_rows", [P, GROUP, D])
        v_rows = sb("v_rows", [P, GROUP, D])
        work = sb("work", [P, 13, 1024])
        gain_mix = sb("gain_mix", [P, D])
        gain_ffn = sb("gain_ffn", [P, D])
        gm_row = sb("gm_row", [P, GM_G * GM_D])
        ret_row = sb("ret_row", [P, RH * RV])
        lat_row = gm_row
        ident = sb("ident", [P, P])
        zeros = sb("zeros", [P, P])
        rope_ret = sb("rope_ret", [P, BLOCKS, 2, RQK // 2])
        rope_mla = sb("rope_mla", [P, BLOCKS, 2, ROPE // 2])
        decay = sb("decay", [P, RH, P])
        q_decay = sb("q_decay", [P, RH, P])
        k_decay = sb("k_decay", [P, RH])
        decay_row = decay[:].rearrange("p r k -> p (r k)")
        causal = sb("causal", [P, P])
        iota = sb("iota", [P, TOPK])
        wsT = sb("wsT", [P, GM_G, P])
        bsT = sb("bsT", [P, GM_G])
        keysT = sb("keysT", [P, LAYERS * 2, NKEYS])
        krT = sb("krT", [ROPE, BLOCKS * P])
        sums = sb("sums", [P, 8])
        roots = sb("roots", [P, 8])
        rstd = sb("rstd", [P, 8])
        att_max = sb("att_max", [P, MH])
        att_bias = sb("att_bias", [P, MH])
        att_sum = sb("att_sum", [P, MH])
        att_inv = sb("att_inv", [P, MH])
        kr = sb("kr", [P, ROPE])
        top_v = sb("top_v", [P, 2 * QH, TOPK])
        top_i = sb("top_i", [P, 2 * QH, TOPK], U32)
        top_f = sb("top_f", [P, 2 * QH, TOPK])
        best_v = sb("best_v", [P, QH, TOPK])
        best_i = sb("best_i", [P, QH, TOPK], U32)
        side_u = sb("side_u", [P, 2, QP], U32)
        side_f = sb("side_f", [P, 2, QP])
        side_e = sb("side_e", [P, 2, QP])
        logits = sb("logits", [P, PH, TOPK])
        gate_sum = sb("gate_sum", [P, QH])
        gates = sb("gates", [P, 2, PICKS])
        experts = sb("experts", [P, 2, PICKS], U32)
        picked = sb("picked", [P, 2, GROUP], U32)
        dots = sb("dots", [P, GROUP])
        gelus = sb("gelus", [P, GROUP])
        pick_w = sb("pick_w", [P, GROUP])
        diag = sb("diag", [P, DIAGS, P])

        def area(i, n=1):
            return work[:, i:i + n, :].rearrange("p a n -> p (a n)")

        hT = area(0)
        gm_u, gm_v, qk, ret_v, gate, qkT = (area(i) for i in range(1, 7))
        sT, decayed = area(7)[:, 0:512], area(7)[:, 512:1024]
        y = area(8, 2)
        yT = area(10, 2)
        ret_o, junk0 = qk, area(11)
        state = area(12)
        cn, cT, qr, qrT, qnT = (area(i) for i in range(1, 6))
        att = area(6, 2).rearrange("p (h k) -> p h k", h=MH)
        pT = area(3, 2)
        att_o, oT = area(1), area(2)
        knT = area(9, 2).rearrange("p (h k) -> p h k", h=MH)
        vals = area(11, 2).rearrange("p (b n) -> p b n", b=BLOCKS)
        junk = area(8)
        route_at = (8, 1)
        scratch = [area(i + 2) for i in route_at]
        qry = [area(i, 2) for i in route_at]
        qryT = area(7)[:, 0:512]
        sc_rest = found = [t[:, 0:512] for t in scratch]
        cand = ones = [t[:, 512:1024] for t in scratch]

        ring = ctx.enter_context(nc.psum_tensor("ring", [P, RING, BANK], F32))
        moe = ctx.enter_context(nc.psum_tensor("moe", [P, D], F32))

        ident_landed = sem("ident_landed")
        rope_landed = sem("rope_landed")
        consts_landed = sem("consts_landed")
        late_landed = sem("late_landed")
        x_landed = sem("x_landed")
        gain_mix_landed = sem("gain_mix_landed")
        gain_ffn_landed = sem("gain_ffn_landed")
        lat_landed = sem("lat_landed")
        w_landed = [sem(f"w_landed{i}") for i in range(W_SLOTS)]
        psum_full = [sem(f"psum_full{i}") for i in range(RING)]
        psum_evac = [sem(f"psum_evac{i}") for i in range(RING)]
        ws_masked = sem("ws_masked")
        zeros_set = sem("zeros_set")
        normed = sem("normed")
        vec_step = sem("vec_step")
        sums_set = sem("sums_set")
        roots_set = sem("roots_set")
        roped = sem("roped")
        v_normed = sem("v_normed")
        decayed_set = sem("decayed_set")
        c_set = sem("c_set")
        qr_set = sem("qr_set")
        max_set = sem("max_set")
        probs_set = sem("probs_set")
        logits_set = sem("logits_set")
        exp_set = sem("exp_set")
        experts_set = sem("experts_set")
        picked_set = sem("picked_set")
        u_landed = [sem(f"u_landed{i}") for i in range(GROUP)]
        v_landed = [sem(f"v_landed{i}") for i in range(GROUP)]
        gathers_begun = sem("gathers_begun")
        u_free = sem("u_free")
        te_used = sem("te_used")
        ve_used = sem("ve_used")
        gelus_set = sem("gelus_set")
        pick_w_set = sem("pick_w_set")
        diag_set = sem("diag_set")
        moe_full = sem("moe_full")
        moe_added = sem("moe_added")
        final_set = sem("final_set")
        out_landed = sem("out_landed")

        def wait_full(eng, u, name):
            n = PRODUCT[u, name]
            eng.wait_ge(psum_full[n % RING], n // RING + 1)
            return ring[:, n % RING, :]

        def wait_evac(eng, u, *names):
            for name in names:
                n = PRODUCT[u, name]
                eng.wait_ge(psum_evac[n % RING], n // RING + 1)

        def evac_of(u, name):
            return psum_evac[PRODUCT[u, name] % RING]

        def full_of(u, name):
            return psum_full[PRODUCT[u, name] % RING]

        chunks = []

        def rows(w, k0, nk, c0, nc_):
            return w[k0 * P:(k0 + nk) * P, c0:c0 + nc_].rearrange("(k p) n -> p k n", p=P)

        for u in range(UNITS):
            if layer_of(u) == 0:
                for n in IN_ORDER:
                    chunks += [(rows(a["hy_w_in"], k, 4, n * BANK, BANK), u, f"in{n}") for k in (0, 4)]
                for n in range(2):
                    chunks += [(rows(a["hy_w_out"], k, 4, n * BANK, BANK), u, f"out{n}") for k in (0, 4, 8, 12)]
            else:
                chunks += [(rows(a["mla_w_down"], k, 2, 0, DOWN), u, "down1") for k in range(0, KD, 2)]
                chunks += [(rows(a["mla_w_q_up"], k, 1, 0, MH * QKD), u, "qn1") for k in range(QR // P)]
                chunks += [(rows(a["mla_w_kv_up"], k, 1, 0, MH * 2 * NOPE), u, "v1") for k in range(KVR // P)]
                for n in range(2):
                    chunks += [(rows(a["mla_w_out"], k, 4, n * BANK, BANK), u, f"out{n}") for k in (0, 4)]
            for n in range(4):
                chunks += [(rows(a["peer_w_q"][layer_of(u)], k, 4, n * BANK, BANK), u, f"q{n}") for k in (0, 4)]

        def chunk_tile(i):
            src = chunks[i][0]
            nk, n = src.shape[1], src.shape[2]
            return w_ring[:, i % W_SLOTS, 0:nk * n].rearrange("p (k n) -> p k n", k=nk)

        early = [(decay[:], a["c_decay"]),
                 (k_decay[:], a["c_k_decay"]), (bsT[:], a["gm_b_sT"]),
                 (gm_row[:], a["gm_v_norm"].broadcast_to([P, D])), (wsT[:], a["gm_w_sT"])]
        late = [(ret_row[:], a["ret_norm"].broadcast_to([P, D])), (q_decay[:], a["c_q_decay"]),
                (keysT[:], a["peer_keysT"]), (iota[:], a["c_iota"]), (rope_mla[:], a["c_rope_mla"]),
                (causal[:], a["c_causal"])]

        block = ctx.enter_context(nc.Block())

        @block.sync
        def _(sp):
            sp.dma_start(x[:, 0, :], a["x"][0:P, :]).then_inc(x_landed, 16)
            sp.dma_start(gain_mix[:], a["norm_mix"][0:1, :].broadcast_to([P, D])).then_inc(gain_mix_landed, 16)
            for i, (src, u, name) in enumerate(chunks):
                first = i == 0 or chunks[i - 1][1] != u
                if first and u == BLOCKS:
                    sp.wait_ge(normed, 2 * (BLOCKS - 1) + 1)
                    sp.dma_start(gain_mix[:], a["norm_mix"][1:2, :].broadcast_to([P, D])).then_inc(gain_mix_landed, 16)
                    sp.wait_ge(v_normed, BLOCKS)
                    sp.dma_start(lat_row[:, 0:QR], a["mla_q_norm"].broadcast_to([P, QR])).then_inc(lat_landed, 16)
                    sp.dma_start(lat_row[:, QR:QR + KVR], a["mla_kv_norm"].broadcast_to([P, KVR])).then_inc(lat_landed, 16)
                if i >= W_SLOTS:
                    _, uu, last_user = chunks[i - W_SLOTS]
                    wait_full(sp, uu, last_user)
                sp.dma_start(chunk_tile(i), src).then_inc(w_landed[i % W_SLOTS], 16)
                if i == W_SLOTS - 1:
                    sp.dma_start(gain_ffn[:], a["norm_ffn"][0:1, :].broadcast_to([P, D])).then_inc(gain_ffn_landed, 16)
                    sp.dma_start(x[:, 1, :], a["x"][P:2 * P, :]).then_inc(x_landed, 16)
                if name == "out0" and u == BLOCKS and chunks[i - 1][2] != "out0":
                    sp.wait_ge(normed, 2 * BLOCKS)
                    sp.dma_start(gain_ffn[:], a["norm_ffn"][1:2, :].broadcast_to([P, D])).then_inc(gain_ffn_landed, 16)
            sp.wait_ge(normed, 2 * UNITS - 1)
            sp.dma_start(gain_mix[:], a["final_norm"].broadcast_to([P, D])).then_inc(gain_mix_landed, 16)
            for b in range(BLOCKS):
                sp.wait_ge(final_set, b + 1)
                sp.dma_start(out[b * P:(b + 1) * P, :], h[:, b, :]).then_inc(out_landed, 16)
            sp.wait_ge(out_landed, 16 * BLOCKS)

        @block.gpsimd
        def _(pool):
            pool.dma_start(ident[:], a["c_ident"]).then_inc(ident_landed, 16)
            pool.dma_start(rope_ret[:], a["c_rope_ret"]).then_inc(rope_landed, 16)
            pool.wait_ge(rope_landed, 16)
            for dst, src in early:
                pool.dma_start(dst, src).then_inc(consts_landed, 16)
            for dst, src in late:
                pool.dma_start(dst, src).then_inc(late_landed, 16)
            pool.wait_ge(consts_landed, 16 * len(early))
            nc.gpsimd.affine_select(out=wsT[:], in_=wsT[:], compare_op=ALU.is_ge, fill=0.0, base=0,
                                    pattern=[[0, GM_G], [1, P]], channel_multiplier=-1).then_inc(ws_masked, 1)

            def gather(rows_sb, table, k, half, landed):
                pool.sem_inc(gathers_begun, 1)
                pool.indirect_dma_start(rows_sb[:, k, :], None, table,
                                        bass.IndirectOffsetOnAxis(picked[:, half, k:k + 1], 0)).then_inc(landed[k], 16)

            def gather_quarter(u, quarter):
                pool.wait_ge(experts_set, u * QUARTERS + quarter + 1)
                with nc.gpsimd.Fori(0, QP // GROUP // 2) as i:
                    for half in range(2):
                        g0 = quarter * (QP // GROUP) + half
                        group = i * 2 + (u * GROUPS + g0)
                        nc.gpsimd.tensor_copy(picked[:, half, :],
                                              experts[:, u % 2, bass.ds(i * 2 * GROUP + g0 * GROUP, GROUP)]
                                              ).then_inc(picked_set, 1)
                        pool.wait_ge(picked_set, group + 1)
                        for k in range(GROUP):
                            pool.wait_ge(u_free, group * GROUP + (k + 1))
                            gather(u_rows, a["peer_u"], k, half, u_landed)
                        for k in range(GROUP):
                            if k < TE_PICKS:
                                pool.wait_ge(te_used, group * TE_PICKS + (k + 1))
                            else:
                                pool.wait_ge(ve_used, group * VE_PICKS + (k - TE_PICKS + 1))
                            gather(v_rows, a["peer_v"], k, half, v_landed)

            for u in range(UNITS):
                for quarter in range(QUARTERS):
                    gather_quarter(u, quarter)

        @block.tensor
        def _(pe):
            at = [0]

            def fill(u, name):
                n = PRODUCT[u, name]
                if n >= RING:
                    pe.wait_ge(psum_evac[n % RING], n // RING)
                return ring[:, n % RING, :]

            def next_chunk():
                i = at[0]
                at[0] += 1
                pe.wait_ge(w_landed[i % W_SLOTS], 16 * (i // W_SLOTS + 1))
                return chunk_tile(i)

            def transposes(u, name, src, count, width=P):
                bank = fill(u, name)
                for j in range(count):
                    last = nc.tensor.transpose(bank[0:width, j * P:(j + 1) * P], src[:, j * width:(j + 1) * width], ident[:])
                last.then_inc(full_of(u, name), 1)

            def project(u, name, actT, steps):
                bank = fill(u, name)
                for k in range(steps):
                    if k % 4 == 0:
                        w = next_chunk()
                    last = nc.tensor.matmul(bank, actT[:, k * P:(k + 1) * P], w[:, k % 4, :],
                                            start=k == 0, stop=k == steps - 1)
                last.then_inc(full_of(u, name), 1)

            def mixer0(u):
                b = block_of(u)
                yield -1
                pe.wait_ge(ident_landed, 16)
                pe.wait_ge(normed, 2 * u + 1)
                for i in range(2):
                    transposes(u, f"hT{i}", h[:, u % 2, i * 512:(i + 1) * 512], 4)
                wait_evac(pe, u, "hT0", "hT1")
                for n in (4, 5):
                    project(u, f"in{n}", hT, KD)
                yield 0
                for n in (6, 7):
                    project(u, f"in{n}", hT, KD)
                yield 1
                pe.wait_ge(roped, 2 * (u + 1))
                for i in range(2):
                    transposes(u, f"qkT{i}", qk[:, i * 512:(i + 1) * 512], RH)
                for n in (8, 9):
                    project(u, f"in{n}", hT, KD)
                wait_evac(pe, u, "qkT0", "qkT1")
                bank = fill(u, "ret_s")
                for r in range(RH):
                    last = nc.tensor.matmul(bank[:, r * P:(r + 1) * P], qkT[:, 512 + r * P:512 + (r + 1) * P],
                                            qkT[:, r * P:(r + 1) * P], start=True, stop=True)
                last.then_inc(full_of(u, "ret_s"), 1)
                yield 2
                for n in (2, 3):
                    project(u, f"in{n}", hT, KD)
                wait_evac(pe, u, "in6", "in7", "ret_s")
                pe.wait_ge(decayed_set, u + 1)
                for i in range(2):
                    bank = fill(u, f"ret_o{i}")
                    for j in range(2):
                        r = 2 * i + j
                        part = bank[:, j * RV:(j + 1) * RV]
                        last = nc.tensor.matmul(part, sT[:, r * P:(r + 1) * P], ret_v[:, r * RV:(r + 1) * RV],
                                                start=True, stop=b == 0)
                        if b == 1:
                            last = nc.tensor.matmul(part, decayed[:, r * P:(r + 1) * P], state[:, r * RV:(r + 1) * RV],
                                                    start=False, stop=True)
                    last.then_inc(full_of(u, f"ret_o{i}"), 1)
                if b == 0:
                    for i in range(2):
                        bank = fill(u, f"st{i}")
                        for j in range(2):
                            r = 2 * i + j
                            last = nc.tensor.matmul(bank[:, j * RV:(j + 1) * RV], decayed[:, r * P:(r + 1) * P],
                                                    ret_v[:, r * RV:(r + 1) * RV], start=True, stop=True)
                        last.then_inc(full_of(u, f"st{i}"), 1)
                yield 3
                for n in (0, 1):
                    project(u, f"in{n}", hT, KD)
                yield 4
                pe.wait_ge(v_normed, u + 1)
                pe.wait_ge(ws_masked, 1)
                for i in range(2):
                    bank = fill(u, f"mix{i}")
                    for j in range(2):
                        g = 2 * i + j
                        last = nc.tensor.matmul(bank[:, j * GM_D:(j + 1) * GM_D], wsT[:, g, :],
                                                gm_v[:, g * GM_D:(g + 1) * GM_D], start=True, stop=True)
                    last.then_inc(full_of(u, f"mix{i}"), 1)
                yield 5
                wait_evac(pe, u, "mix0", "mix1")
                for i in range(4):
                    transposes(u, f"yT{i}", y[:, i * 512:(i + 1) * 512], 4)
                wait_evac(pe, u, "yT0", "yT1", "yT2", "yT3")
                for i in range(2):
                    yield 5 + i
                    project(u, f"out{i}", yT, 2 * KD)

            def mixer1(u):
                b = block_of(u)
                keys = (b + 1) * P
                yield 0
                pe.wait_ge(normed, 2 * u + 1)
                for i in range(2):
                    transposes(u, f"hT{i}", h[:, u % 2, i * 512:(i + 1) * 512], 4)
                wait_evac(pe, u, "hT0", "hT1")
                down0, down1 = fill(u, "down0"), fill(u, "down1")
                for k in range(KD):
                    if k % 2 == 0:
                        w = next_chunk()
                    first = nc.tensor.matmul(down0[:, 0:QR], hT[:, k * P:(k + 1) * P], w[:, k % 2, 0:QR],
                                             start=k == 0, stop=k == KD - 1)
                    last = nc.tensor.matmul(down1[:, 0:DOWN - QR], hT[:, k * P:(k + 1) * P], w[:, k % 2, QR:DOWN],
                                            start=k == 0, stop=k == KD - 1)
                first.then_inc(full_of(u, "down0"), 1)
                last.then_inc(full_of(u, "down1"), 1)
                yield 2
                pe.wait_ge(c_set, (u - BLOCKS) + 1)
                transposes(u, "cT0", cn, QR // P)
                transposes(u, "cT1", cn[:, QR:QR + KVR], KVR // P)
                transposes(u, "krT", kr[:], 1, ROPE)
                wait_evac(pe, u, "cT0", "cT1")
                wq = [next_chunk()[:, 0, :] for _ in range(QR // P)]
                heads = [w.rearrange("p (m n) -> p m n", m=MH) for w in wq]
                bank = fill(u, "qr")
                for k in range(QR // P):
                    last = nc.tensor.matmul(bank, cT[:, k * P:(k + 1) * P], heads[k][:, :, NOPE:QKD],
                                            start=k == 0, stop=k == QR // P - 1)
                last.then_inc(full_of(u, "qr"), 1)
                for i in range(2):
                    bank = fill(u, f"qn{i}")
                    for j in range(4):
                        for k in range(QR // P):
                            last = nc.tensor.matmul(bank[:, j * P:(j + 1) * P], heads[k][:, 4 * i + j, 0:NOPE],
                                                    cT[:, k * P:(k + 1) * P], start=k == 0, stop=k == QR // P - 1)
                    last.then_inc(full_of(u, f"qn{i}"), 1)
                kvT = cT[:, QR:QR + KVR]
                wkv = [next_chunk()[:, 0, :].rearrange("p (m n) -> p m n", m=MH) for _ in range(KVR // P)]
                for i in range(2):
                    bank = fill(u, f"kn{i}")
                    for j in range(4):
                        for k in range(KVR // P):
                            last = nc.tensor.matmul(bank[:, j * P:(j + 1) * P], wkv[k][:, 4 * i + j, 0:NOPE],
                                                    kvT[:, k * P:(k + 1) * P], start=k == 0, stop=k == KVR // P - 1)
                    last.then_inc(full_of(u, f"kn{i}"), 1)
                yield 3
                for i in range(2):
                    bank = fill(u, f"v{i}")
                    for k in range(KVR // P):
                        last = nc.tensor.matmul(bank, kvT[:, k * P:(k + 1) * P], wkv[k][:, 4 * i:4 * i + 4, NOPE:2 * NOPE],
                                                start=k == 0, stop=k == KVR // P - 1)
                    last.then_inc(full_of(u, f"v{i}"), 1)
                pe.wait_ge(qr_set, (u - BLOCKS) + 1)
                for i in range(2):
                    transposes(u, f"qrT{i}", qr[:, i * 4 * ROPE:(i + 1) * 4 * ROPE], 4, ROPE)
                wait_evac(pe, u, "krT", "qn0", "qn1", "kn0", "kn1", "qrT0", "qrT1")
                per = BANK // keys
                for i in range(MH // per):
                    bank = fill(u, f"s{i}")
                    for j in range(per):
                        m = i * per + j
                        part = bank[:, j * keys:(j + 1) * keys]
                        nc.tensor.matmul(part, qnT[:, m * P:(m + 1) * P], knT[:, m, 0:keys], start=True, stop=False)
                        last = nc.tensor.matmul(part, qrT[0:ROPE, m * P:(m + 1) * P], krT[:, 0:keys], start=False, stop=True)
                    last.then_inc(full_of(u, f"s{i}"), 1)
                yield 4
                pe.wait_ge(probs_set, (u - BLOCKS) + 1)
                for i in range(2 * (b + 1)):
                    bank = fill(u, f"pT{i}")
                    for j in range(4):
                        m, kb = divmod(4 * i + j, b + 1)
                        last = nc.tensor.transpose(bank[:, j * P:(j + 1) * P], att[:, m, kb * P:(kb + 1) * P], ident[:])
                    last.then_inc(full_of(u, f"pT{i}"), 1)
                wait_evac(pe, u, "v0", "v1", *[f"pT{i}" for i in range(2 * (b + 1))])
                for i in range(2):
                    bank = fill(u, f"o{i}")
                    for j in range(4):
                        m = 4 * i + j
                        for kb in range(b + 1):
                            n = m * (b + 1) + kb
                            last = nc.tensor.matmul(bank[:, j * P:(j + 1) * P], pT[:, n * P:(n + 1) * P],
                                                    vals[:, kb, m * MV:(m + 1) * MV], start=kb == 0, stop=kb == b)
                    last.then_inc(full_of(u, f"o{i}"), 1)
                yield 5
                wait_evac(pe, u, "o0", "o1")
                for i in range(2):
                    transposes(u, f"oT{i}", att_o[:, i * 512:(i + 1) * 512], 4)
                wait_evac(pe, u, "oT0", "oT1")
                for i in range(2):
                    project(u, f"out{i}", oT, KD)

            def route(u, at_group):
                lay = layer_of(u)
                yield at_group
                if u == 0:
                    pe.wait_ge(late_landed, 16 * len(late))
                pe.wait_ge(normed, 2 * u + 2)
                for i in range(2):
                    transposes(u, f"fT{i}", h[:, u % 2, i * 512:(i + 1) * 512], 4)
                wait_evac(pe, u, "fT0", "fT1")
                for i in range(QUARTERS):
                    yield at_group + i // 2
                    project(u, f"q{i}", hT, KD)
                    wait_evac(pe, u, f"q{i}")
                    transposes(u, f"qT{i}", qry[lay][:, i * 512:(i + 1) * 512], 4)
                    wait_evac(pe, u, f"qT{i}")
                    bank = fill(u, f"sc{i}")
                    for j in range(2 * QH):
                        last = nc.tensor.matmul(bank[:, j * P:(j + 1) * P], qryT[:, j * P:(j + 1) * P],
                                                keysT[:, lay * 2 + j % 2, :], start=True, stop=True)
                    last.then_inc(full_of(u, f"sc{i}"), 1)

            def stages_of(u):
                if u >= UNITS:
                    return
                if layer_of(u) == 0:
                    yield from mixer0(u)
                    yield from route(u, 8)
                else:
                    yield from mixer1(u)
                    yield from route(u, 7)

            def begin(u):
                pe.wait_ge(zeros_set, 1)
                if u == 0:
                    pe.wait_ge(consts_landed, 16 * len(early))
                else:
                    pe.wait_ge(moe_added, u)
                for c in range(2):
                    nc.tensor.matmul(moe[:, c * BANK:(c + 1) * BANK], zeros[:], decay_row,
                                     start=True, stop=False, skip_group_check=True)

            def group_of_picks(u, g, first):
                group = g + u * GROUPS
                for k in range(TE_PICKS):
                    pe.wait_ge(diag_set, group * TE_PICKS + (k + 1))
                    pe.wait_ge(v_landed[k], group * 16 + 16)
                    for c in range(2):
                        last = nc.tensor.matmul(moe[:, c * BANK:(c + 1) * BANK], diag[:, k, :],
                                                v_rows[:, k, c * BANK:(c + 1) * BANK],
                                                start=False, stop=False, skip_group_check=True)
                    last.then_inc(te_used, 1)

            def end(u):
                for c in range(2):
                    last = nc.tensor.matmul(moe[:, c * BANK:(c + 1) * BANK], zeros[:], decay_row,
                                            start=False, stop=True, skip_group_check=True)
                last.then_inc(moe_full, 1)

            interleave(nc.tensor, stages_of, lambda u: iter(()), begin, group_of_picks, end)

        @block.scalar
        def _(act):
            def evacuate(u, name, dst, func=ACT.Copy, width=BANK, parts=P):
                bank = wait_full(act, u, name)
                nc.scalar.activation(dst, bank[0:parts, 0:width], func).then_inc(evac_of(u, name), 1)

            norms = [0]

            def take_roots(n):
                norms[0] += 1
                act.wait_ge(sums_set, norms[0])
                nc.scalar.activation(roots[:, 0:n], sums[:, 0:n], ACT.Sqrt).then_inc(roots_set, 1)

            def half(t, i, n=BANK):
                return t[:, i * n:(i + 1) * n]

            def mixer0(u):
                yield -1
                take_roots(1)
                for i in range(2):
                    evacuate(u, f"hT{i}", half(hT, i))
                yield 0
                for i in range(2):
                    evacuate(u, f"in{6 + i}", half(ret_v, i))
                yield 1
                for i in range(2):
                    evacuate(u, f"qkT{i}", half(qkT, i))
                for i in range(2):
                    evacuate(u, f"in{8 + i}", half(gate, i), ACT.Silu)
                yield 2
                for i in range(2):
                    evacuate(u, f"in{2 + i}", half(gm_v, i), ACT.Gelu)
                for i in range(2):
                    evacuate(u, f"ret_o{i}", half(ret_o, i))
                if block_of(u) == 0:
                    for i in range(2):
                        evacuate(u, f"st{i}", half(state, i))
                yield 3
                take_roots(RH + GM_G)
                for i in range(2):
                    evacuate(u, f"in{i}", half(gm_u, i), ACT.Gelu)
                yield 5
                for i in range(4):
                    evacuate(u, f"yT{i}", half(yT, i))

            def mixer1(u):
                b = block_of(u)
                yield -1
                take_roots(1)
                yield 0
                for i in range(2):
                    evacuate(u, f"hT{i}", half(hT, i))
                evacuate(u, "down0", cn[:, 0:QR], width=QR)
                evacuate(u, "down1", cn[:, QR:DOWN], width=DOWN - QR)
                yield 1
                take_roots(2)
                yield 2
                evacuate(u, "cT0", cT[:, 0:QR], width=QR)
                evacuate(u, "cT1", cT[:, QR:QR + KVR], width=KVR)
                evacuate(u, "krT", krT[:, b * P:(b + 1) * P], width=P, parts=ROPE)
                for i in range(2):
                    evacuate(u, f"qn{i}", half(qnT, i))
                for i in range(2):
                    bank = wait_full(act, u, f"kn{i}")
                    nc.scalar.activation(knT[:, 4 * i:4 * i + 4, b * P:(b + 1) * P],
                                         bank.rearrange("p (m k) -> p m k", m=4), ACT.Copy).then_inc(evac_of(u, f"kn{i}"), 1)
                yield 3
                for i in range(2):
                    evacuate(u, f"v{i}", vals[:, b, i * BANK:(i + 1) * BANK])
                for i in range(2):
                    evacuate(u, f"qrT{i}", qrT[0:ROPE, i * BANK:(i + 1) * BANK], parts=ROPE)
                yield 4
                act.wait_ge(max_set, (u - BLOCKS) + 1)
                for m in range(MH):
                    part = att[:, m, 0:(b + 1) * P]
                    last = nc.scalar.activation(part, part, ACT.Exp, bias=att_bias[:, m:m + 1], scale=ATT_SCALE,
                                                accum_out=att_sum[:, m:m + 1])
                last.then_inc(probs_set, 1)
                for i in range(2 * (b + 1)):
                    evacuate(u, f"pT{i}", half(pT, i))
                yield 5
                for i in range(2):
                    evacuate(u, f"oT{i}", half(oT, i))

            def route(u, at_group):
                yield at_group - 1
                take_roots(1)
                yield at_group
                for i in range(2):
                    evacuate(u, f"fT{i}", half(hT, i))
                lay = layer_of(u)
                for i in range(QUARTERS):
                    yield at_group + i // 2
                    evacuate(u, f"q{i}", half(qry[lay], i))
                    evacuate(u, f"qT{i}", qryT)
                    evacuate(u, f"sc{i}", half(qry[lay], i))
                    if u == 0 and i == 1:
                        take_exp(u, 0)
                if u:
                    yield at_group + 2
                    take_exp(u, 0)
                    yield from rest_of_route(u, at_group + 3)

            def take_exp(u, q):
                act.wait_ge(logits_set, u * QUARTERS + q + 1)
                part = logits[:, q * QH:(q + 1) * QH, :]
                nc.scalar.activation(part, part, ACT.Exp).then_inc(exp_set, 1)

            def rest_of_route(u, at_group):
                for q in range(1, QUARTERS):
                    yield at_group + 2 * q - 1
                    take_exp(u, q)

            def stages_of(u):
                if u >= UNITS:
                    yield -1
                    take_roots(1)
                elif layer_of(u) == 0:
                    yield from mixer0(u)
                    yield from route(u, 8)
                else:
                    yield from mixer1(u)
                    yield from route(u, 7)

            def group_of_picks(u, g, first):
                group = g + u * GROUPS
                act.wait_ge(u_free, group * GROUP + 2 * GROUP)
                nc.scalar.activation(gelus[:], dots[:], ACT.Gelu).then_inc(gelus_set, 1)
                act.wait_ge(pick_w_set, group + 1)
                if first and u == 0:
                    act.wait_ge(ident_landed, 16)
                for k in range(TE_PICKS):
                    act.wait_ge(te_used, group * TE_PICKS + (k + 1))
                    nc.scalar.mul(diag[:, k, :], ident[:], pick_w[:, k:k + 1]).then_inc(diag_set, 1)

            interleave(nc.scalar, stages_of, lambda u: rest_of_route(u, 0), lambda u: None, group_of_picks, lambda u: None)

        @block.vector
        def _(dve):
            steps, norms = [0], [0]

            def step_done(ins):
                ins.then_inc(vec_step, 1)
                steps[0] += 1
                dve.wait_ge(vec_step, steps[0])

            nc.vector.memset(zeros[:], 0.0).then_inc(zeros_set, 1)

            def mean_squares(parts, scratch):
                at = 0
                for i, part in enumerate(parts):
                    if at == D:
                        step_done(last)
                        at = 0
                    width = part.shape[1]
                    last = nc.vector.tensor_tensor_reduce(out=scratch[:, at:at + width], in0=part, in1=part, scale=1.0 / width,
                                                          scalar=EPS, op0=ALU.mult, op1=ALU.add, accum_out=sums[:, i:i + 1])
                    at += width
                last.then_inc(sums_set, 1)

            def inverse_roots(n):
                norms[0] += 1
                dve.wait_ge(roots_set, norms[0])
                step_done(nc.vector.reciprocal(rstd[:, 0:n], roots[:, 0:n]))

            def norm_tokens(src, gain, dst):
                inverse_roots(1)
                return nc.vector.scalar_tensor_tensor(out=dst, in0=src, scalar=rstd[:, 0:1], in1=gain,
                                                      op0=ALU.mult, op1=ALU.mult)

            def add_output(u):
                for i in range(2):
                    bank = wait_full(dve, u, f"out{i}")
                    part = x[:, block_of(u), i * BANK:(i + 1) * BANK]
                    nc.vector.tensor_tensor(part, bank, part, ALU.add).then_inc(evac_of(u, f"out{i}"), 1)
                wait_evac(dve, u, "out0", "out1")

            def rotate(u, name, dst, table, heads, half, scratch, src=None):
                bank = (wait_full(dve, u, name) if src is None else src)
                width = heads * 2 * half
                v = bank[:, 0:width].rearrange("p (n k) -> p n k", k=half)
                cos = table[:, 0, :].unsqueeze(1).broadcast_to([P, 2 * heads, half])
                sin = table[:, 1, :].unsqueeze(1).broadcast_to([P, 2 * heads, half])
                d = dst[:, 0:width].rearrange("p (n k) -> p n k", k=half)
                t = scratch[:, 0:width].rearrange("p (n k) -> p n k", k=half)
                by_cos = nc.vector.tensor_tensor(d, v, cos, ALU.mult)
                by_sin = nc.vector.tensor_tensor(t, v, sin, ALU.mult)
                if src is None:
                    by_sin.then_inc(evac_of(u, name), 1)
                    wait_evac(dve, u, name)
                else:
                    step_done(by_sin)
                d4 = dst[:, 0:width].rearrange("p (n s k) -> p n s k", s=2, k=half)
                t4 = scratch[:, 0:width].rearrange("p (n s k) -> p n s k", s=2, k=half)
                nc.vector.tensor_tensor(d4[:, :, 0, :], d4[:, :, 0, :], t4[:, :, 1, :], ALU.subtract)
                return nc.vector.tensor_tensor(d4[:, :, 1, :], d4[:, :, 1, :], t4[:, :, 0, :], ALU.add)

            def mixer0(u):
                b = block_of(u)
                yield -1
                if b == 0:
                    dve.wait_ge(x_landed, 16)
                    dve.wait_ge(gain_mix_landed, 16)
                else:
                    dve.wait_ge(x_landed, 32)
                mean_squares([x[:, b, :]], junk0)
                norm_tokens(x[:, b, :], gain_mix[:], h[:, u % 2, :]).then_inc(normed, 1)
                yield 0
                if u == 0:
                    dve.wait_ge(rope_landed, 16)
                rotate(u, "in4", qk[:, 0:512], rope_ret[:, b], RH, RQK // 2, junk0).then_inc(roped, 1)
                dve.wait_ge(roped, 2 * u + 1)
                rotate(u, "in5", qk[:, 512:1024], rope_ret[:, b], RH, RQK // 2, junk0).then_inc(roped, 1)
                dve.wait_ge(roped, 2 * u + 2)
                if u == 0:
                    dve.wait_ge(consts_landed, 16 * len(early))
                if b == 0:
                    nc.vector.tensor_tensor(decayed.rearrange("p (r k) -> p r k", r=RH),
                                            qk[:, 512:1024].rearrange("p (r k) -> p r k", r=RH),
                                            k_decay[:].unsqueeze(2).broadcast_to([P, RH, P]), ALU.mult
                                            ).then_inc(decayed_set, 1)
                yield 2
                if b == 1:
                    wait_evac(dve, u, "qkT0")
                    nc.vector.tensor_tensor(decayed.rearrange("p (r k) -> p r k", r=RH),
                                            qkT[:, 0:512].rearrange("p (r k) -> p r k", r=RH), q_decay[:], ALU.mult
                                            ).then_inc(decayed_set, 1)
                bank = wait_full(dve, u, "ret_s")
                nc.vector.tensor_tensor(sT.rearrange("p (r k) -> p r k", r=RH), bank.rearrange("p (r k) -> p r k", r=RH),
                                        decay[:], ALU.mult).then_inc(evac_of(u, "ret_s"), 1)
                wait_evac(dve, u, "in8", "in9")
                if u == 0:
                    dve.wait_ge(late_landed, 16 * len(late))
                step_done(nc.vector.tensor_tensor(gate, gate, ret_row[:], ALU.mult))
                yield 3
                wait_evac(dve, u, "ret_o0", "ret_o1", "in2", "in3")
                mean_squares([ret_o[:, r * RV:(r + 1) * RV] for r in range(RH)]
                             + [gm_v[:, g * GM_D:(g + 1) * GM_D] for g in range(GM_G)], junk0)
                yield 4
                inverse_roots(RH + GM_G)
                for g in range(GM_G):
                    part = gm_v[:, g * GM_D:(g + 1) * GM_D]
                    last = nc.vector.scalar_tensor_tensor(out=part, in0=part, scalar=rstd[:, RH + g:RH + g + 1],
                                                          in1=gm_row[:, g * GM_D:(g + 1) * GM_D], op0=ALU.mult, op1=ALU.mult)
                last.then_inc(v_normed, 1)
                yield 5
                for r in range(RH):
                    nc.vector.scalar_tensor_tensor(out=y[:, 1024 + r * RV:1024 + (r + 1) * RV], in0=ret_o[:, r * RV:(r + 1) * RV],
                                                   scalar=rstd[:, r:r + 1], in1=gate[:, r * RV:(r + 1) * RV],
                                                   op0=ALU.mult, op1=ALU.mult)
                wait_evac(dve, u, "in0", "in1")
                for i in range(2):
                    bank = wait_full(dve, u, f"mix{i}")
                    for j in range(2):
                        g = 2 * i + j
                        last = nc.vector.scalar_tensor_tensor(out=y[:, g * GM_D:(g + 1) * GM_D], in0=bank[:, j * GM_D:(j + 1) * GM_D],
                                                              scalar=bsT[:, g:g + 1], in1=gm_u[:, g * GM_D:(g + 1) * GM_D],
                                                              op0=ALU.add, op1=ALU.mult)
                    last.then_inc(evac_of(u, f"mix{i}"), 1)
                wait_evac(dve, u, "mix0", "mix1")
                yield 7
                add_output(u)

            def mixer1(u):
                b = block_of(u)
                keys = (b + 1) * P
                yield -1
                mean_squares([x[:, b, :]], junk)
                yield 0
                dve.wait_ge(gain_mix_landed, 32)
                norm_tokens(x[:, b, :], gain_mix[:], h[:, u % 2, :]).then_inc(normed, 1)
                yield 1
                wait_evac(dve, u, "down0", "down1")
                mean_squares([cn[:, 0:QR], cn[:, QR:QR + KVR]], junk)
                yield 2
                inverse_roots(2)
                dve.wait_ge(lat_landed, 32)
                for i, (lo, hi) in enumerate(((0, QR), (QR, QR + KVR))):
                    nc.vector.scalar_tensor_tensor(out=cn[:, lo:hi], in0=cn[:, lo:hi], scalar=rstd[:, i:i + 1],
                                                   in1=lat_row[:, lo:hi], op0=ALU.mult, op1=ALU.mult)
                rotate(u, None, kr[:], rope_mla[:, b], 1, ROPE // 2, junk, src=cn[:, QR + KVR:DOWN]).then_inc(c_set, 1)
                yield 3
                rotate(u, "qr", qr[:, 0:512], rope_mla[:, b], MH, ROPE // 2, junk).then_inc(qr_set, 1)
                yield 4
                per = BANK // keys
                for i in range(MH // per):
                    bank = wait_full(dve, u, f"s{i}").rearrange("p (m k) -> p m k", k=keys)
                    rows_of = att[:, i * per:(i + 1) * per, :]
                    if b:
                        nc.vector.tensor_copy(rows_of[:, :, 0:P], bank[:, :, 0:P])
                    nc.vector.tensor_tensor(rows_of[:, :, b * P:keys], bank[:, :, b * P:keys],
                                            causal[:].unsqueeze(1).broadcast_to([P, per, P]), ALU.add
                                            ).then_inc(evac_of(u, f"s{i}"), 1)
                wait_evac(dve, u, *[f"s{i}" for i in range(MH // per)])
                step_done(nc.vector.tensor_reduce(att_max[:], att[:, :, 0:keys], AX, ALU.max))
                nc.vector.tensor_scalar(att_bias[:], att_max[:], -ATT_SCALE, None, ALU.mult).then_inc(max_set, 1)
                yield 5
                dve.wait_ge(probs_set, (u - BLOCKS) + 1)
                step_done(nc.vector.reciprocal(att_inv[:], att_sum[:]))
                for i in range(2):
                    bank = wait_full(dve, u, f"o{i}")
                    nc.vector.tensor_tensor(att_o[:, i * BANK:(i + 1) * BANK].rearrange("p (m k) -> p m k", m=4),
                                            bank.rearrange("p (m k) -> p m k", m=4),
                                            att_inv[:, 4 * i:4 * i + 4].unsqueeze(2).broadcast_to([P, 4, MV]), ALU.mult
                                            ).then_inc(evac_of(u, f"o{i}"), 1)
                yield 6
                add_output(u)

            def best16(values, rest, out_v, out_i):
                n = values.shape[1]
                for j in range(n):
                    last = nc.vector.max(out_v[:, j, 0:8], values[:, j, :])
                step_done(last)
                for j in range(n):
                    nc.vector.max_index(out_i[:, j, 0:8], out_v[:, j, 0:8], values[:, j, :])
                for j in range(n):
                    last = nc.vector.match_replace(rest[:, j, :], out_v[:, j, 0:8], values[:, j, :], LOWEST)
                step_done(last)
                for j in range(n):
                    last = nc.vector.max(out_v[:, j, 8:16], rest[:, j, :])
                step_done(last)
                for j in range(n):
                    last = nc.vector.max_index(out_i[:, j, 8:16], out_v[:, j, 8:16], rest[:, j, :])
                step_done(last)

            def route(u, at_group):
                b, lay, par = block_of(u), layer_of(u), u % 2
                yield at_group - 1
                mean_squares([x[:, b, :]], junk if lay else junk0)
                yield at_group
                dve.wait_ge(gain_ffn_landed, 16 * (lay + 1))
                norm_tokens(x[:, b, :], gain_ffn[:], h[:, par, :]).then_inc(normed, 1)
                yield at_group + 1
                best_of_sides(u, 0)
                yield at_group + 2
                pick_experts(u, 0)
                if u == 0:
                    normalise_gates(u, 0)
                else:
                    yield from rest_of_route(u, at_group + 3)

            def rest_of_route(u, at_group):
                for q in range(1, QUARTERS):
                    yield at_group + 2 * q - 2
                    best_of_sides(u, q)
                    yield at_group + 2 * q - 1
                    pick_experts(u, q)
                    if u or q > 1:
                        normalise_gates(u, q - 1)
                yield at_group + 2 * QUARTERS - 2
                normalise_gates(u, QUARTERS - 1)

            def best_of_sides(u, q):
                wait_evac(dve, u, f"sc{q}")
                lay = layer_of(u)
                sides = qry[lay][:, q * 512:(q + 1) * 512].rearrange("p (j k) -> p j k", k=NKEYS)
                best16(sides, sc_rest[lay].rearrange("p (j k) -> p j k", k=NKEYS), top_v, top_i)
                step_done(nc.vector.tensor_copy(top_f[:], top_i[:]))

            def pick_experts(u, q):
                lay = layer_of(u)
                heads = slice(QH * q, QH * (q + 1))
                picks = slice(QP * q, QP * (q + 1))
                pair = top_v[:].rearrange("p (m s) k -> p m s k", s=2)
                pairs = cand[lay].rearrange("p (m k) -> p m k", m=QH)
                step_done(nc.vector.tensor_tensor(pairs.rearrange("p m (i j) -> p m i j", i=TOPK),
                                                  pair[:, :, 0, :].unsqueeze(3).broadcast_to([P, QH, TOPK, TOPK]),
                                                  pair[:, :, 1, :].unsqueeze(2).broadcast_to([P, QH, TOPK, TOPK]), ALU.add))
                cand_rest = qry[lay][:, q * 512:(q + 1) * 512].rearrange("p (m k) -> p m k", m=QH)
                best16(pairs, cand_rest, best_v, best_i)
                nc.vector.tensor_tensor(logits[:, heads, :], best_v[:], best_v[:, :, 0:1].broadcast_to([P, QH, TOPK]),
                                        ALU.subtract).then_inc(logits_set, 1)
                flat = best_i[:].rearrange("p m k -> p (m k)")
                nc.vector.tensor_scalar(side_u[:, 0, :], flat, 4, None, ALU.logical_shift_right)
                step_done(nc.vector.tensor_scalar(side_u[:, 1, :], flat, TOPK - 1, None, ALU.bitwise_and))
                step_done(nc.vector.tensor_copy(side_f[:], side_u[:]))
                keys = top_f[:].rearrange("p (m s) k -> p m s k", s=2)
                hot, hot_key = (t[lay].rearrange("p (j k) -> p j k", k=TOPK) for t in (ones, found))
                for s in range(2):
                    step_done(nc.vector.tensor_tensor(hot, side_f[:, s, :].unsqueeze(2).broadcast_to([P, QP, TOPK]),
                                                      iota[:].unsqueeze(1).broadcast_to([P, QP, TOPK]), ALU.is_equal))
                    step_done(nc.vector.tensor_tensor(hot_key.rearrange("p (m k) j -> p m k j", m=QH),
                                                      hot.rearrange("p (m k) j -> p m k j", m=QH),
                                                      keys[:, :, s, :].unsqueeze(2).broadcast_to([P, QH, TOPK, TOPK]), ALU.mult))
                    step_done(nc.vector.tensor_reduce(side_e[:, s, :], hot_key, AX, ALU.add))
                step_done(nc.vector.scalar_tensor_tensor(out=side_f[:, 0, :], in0=side_e[:, 0, :], scalar=float(NKEYS),
                                                         in1=side_e[:, 1, :], op0=ALU.mult, op1=ALU.add))
                nc.vector.tensor_scalar(experts[:, u % 2, picks], side_f[:, 0, :], float(layer_of(u) * N_EXPERTS), None,
                                        ALU.add).then_inc(experts_set, 1)
                dve.wait_ge(experts_set, u * QUARTERS + q + 1)

            def normalise_gates(u, q):
                heads = slice(QH * q, QH * (q + 1))
                dve.wait_ge(exp_set, u * QUARTERS + q + 1)
                step_done(nc.vector.tensor_reduce(gate_sum[:], logits[:, heads, :], AX, ALU.add))
                step_done(nc.vector.reciprocal(gate_sum[:], gate_sum[:]))
                step_done(nc.vector.tensor_tensor(gates[:, u % 2, QP * q:QP * (q + 1)].rearrange("p (m k) -> p m k", m=QH),
                                                  logits[:, heads, :], gate_sum[:].unsqueeze(2).broadcast_to([P, QH, TOPK]),
                                                  ALU.mult))

            nc.vector.memset(dots[:, 0:1], 0.0).then_inc(u_free, GROUP)
            nc.vector.memset(dots[:, 1:2], 0.0).then_inc(te_used, TE_PICKS)
            nc.vector.memset(dots[:, 2:3], 0.0).then_inc(ve_used, VE_PICKS)

            def stages_of(u):
                if u >= UNITS:
                    yield -1
                    b = u - UNITS
                    mean_squares([x[:, b, :]], junk)
                    dve.wait_ge(gain_mix_landed, 48)
                    norm_tokens(x[:, b, :], gain_mix[:], h[:, b, :]).then_inc(final_set, 1)
                elif layer_of(u) == 0:
                    yield from mixer0(u)
                    yield from route(u, 8)
                else:
                    yield from mixer1(u)
                    yield from route(u, 7)

            def add_rows(u, group):
                part = x[:, block_of(u), :]
                for k in range(TE_PICKS, GROUP):
                    dve.wait_ge(v_landed[k], group * 16 + 16)
                    nc.vector.scalar_tensor_tensor(out=part, in0=v_rows[:, k, :], scalar=pick_w[:, k:k + 1], in1=part,
                                                   op0=ALU.mult, op1=ALU.add).then_inc(ve_used, 1)
                    dve.wait_ge(ve_used, group * VE_PICKS + (VE_PICKS + k - TE_PICKS + 1))

            def group_of_picks(u, g, first):
                group = g + u * GROUPS
                for k in range(GROUP):
                    dve.wait_ge(u_landed[k], group * 16 + 16)
                    if k == 0 and not (u == 0 and first):
                        dve.wait_ge(gelus_set, group)
                    nc.vector.tensor_tensor_reduce(out=u_rows[:, k, :], in0=u_rows[:, k, :], in1=h[:, u % 2, :],
                                                   scale=1.0, scalar=0.0, op0=ALU.mult, op1=ALU.add,
                                                   accum_out=dots[:, k:k + 1]).then_inc(u_free, 1)
                if not first:
                    add_rows(u, group - 1)
                dve.wait_ge(gelus_set, group + 1)
                if not (u == 0 and first):
                    dve.wait_ge(diag_set, group * TE_PICKS)
                nc.vector.tensor_tensor(pick_w[:], gelus[:], gates[:, u % 2, bass.ds(g * GROUP, GROUP)],
                                        ALU.mult).then_inc(pick_w_set, 1)
                dve.wait_ge(pick_w_set, group + 1)

            def end(u):
                add_rows(u, (u + 1) * GROUPS - 1)
                dve.wait_ge(moe_full, u + 1)
                part = x[:, block_of(u), :]
                nc.vector.tensor_tensor(part, moe[:], part, ALU.add).then_inc(moe_added, 1)
                dve.wait_ge(moe_added, u + 1)

            interleave(nc.vector, stages_of, lambda u: rest_of_route(u, 0), lambda u: None, group_of_picks, end)


def shape_constants():
    f = np.float32
    pos = np.arange(P, dtype=f)
    log_gamma = np.log(f(1.0) - f(2.0) ** (f(-5.0) - np.arange(RH, dtype=f))).astype(f)
    diff = pos[:, None] - pos[None, :]
    scale = f(RQK ** -0.5)
    decay = np.where(diff[None] >= 0, np.exp(diff[None] * log_gamma[:, None, None]), f(0.0)).astype(f) * scale
    q_decay = np.exp((pos[:, None] + f(1.0)) * log_gamma[None, :]).astype(f)
    k_decay = np.exp((f(P) - f(1.0) - pos[:, None]) * log_gamma[None, :]).astype(f) * scale

    def rope(half):
        inv = (f(1.0) / (f(10000.0) ** (np.arange(half, dtype=f) / f(half)))).astype(f)
        ang = np.arange(BLOCKS * P, dtype=f)[:, None] * inv[None, :]
        table = np.stack([np.cos(ang), np.sin(ang)], axis=1).astype(f)
        return np.ascontiguousarray(table.reshape(BLOCKS, P, 2, half).transpose(1, 0, 2, 3))

    return {
        "c_ident": np.eye(P, dtype=f),
        "c_rope_ret": rope(RQK // 2),
        "c_rope_mla": rope(ROPE // 2),
        "c_decay": np.ascontiguousarray(decay.transpose(2, 0, 1)),
        "c_q_decay": np.ascontiguousarray(np.broadcast_to(q_decay.T[None], (P, RH, P))),
        "c_k_decay": k_decay,
        "c_causal": np.where(diff >= 0, f(0.0), f(MASKED)).astype(f),
        "c_iota": np.ascontiguousarray(np.broadcast_to(np.arange(TOPK, dtype=f)[None], (P, TOPK))),
    }


def kernel(x, norm_mix, norm_ffn, hy_w_in, gm_v_norm, gm_w_s, gm_b_s, ret_norm, hy_w_out,
           mla_w_down, mla_q_norm, mla_w_q_up, mla_kv_norm, mla_w_kv_up, mla_w_out,
           peer_w_q, peer_sub_keys, peer_u, peer_v, final_norm):
    import concourse.bacc as bacc
    from concourse.bass_utils import run_bass_kernel_spmd as run

    c = np.ascontiguousarray
    arrays = {
        "x": c(x).reshape(BLOCKS * P, D), "norm_mix": c(norm_mix), "norm_ffn": c(norm_ffn),
        "hy_w_in": c(hy_w_in)[0], "gm_v_norm": c(gm_v_norm), "ret_norm": c(ret_norm), "hy_w_out": c(hy_w_out)[0],
        "gm_w_sT": c(np.transpose(c(gm_w_s)[0], (2, 0, 1))), "gm_b_sT": c(np.transpose(c(gm_b_s)[0])),
        "mla_w_down": c(mla_w_down)[0], "mla_q_norm": c(mla_q_norm), "mla_w_q_up": c(mla_w_q_up)[0],
        "mla_kv_norm": c(mla_kv_norm), "mla_w_kv_up": c(mla_w_kv_up)[0], "mla_w_out": c(mla_w_out)[0],
        "peer_w_q": c(peer_w_q),
        "peer_keysT": c(np.transpose(c(peer_sub_keys).reshape(LAYERS * 2, NKEYS, P), (2, 0, 1))),
        "peer_u": c(peer_u).reshape(LAYERS * N_EXPERTS, D), "peer_v": c(peer_v).reshape(LAYERS * N_EXPERTS, D),
        "final_norm": c(final_norm).reshape(1, D),
    }
    arrays.update(shape_constants())
    nc = bacc.Bacc("TRN2", target_bir_lowering=False, num_devices=1)
    a = {n: nc.dram_tensor("in_" + n, v.shape, F32, kind="ExternalInput").ap() for n, v in arrays.items()}
    out = nc.dram_tensor("out_dram", (BLOCKS * P, D), F32, kind="ExternalOutput").ap()
    build(nc, a, out)
    result = run(nc, [{"in_" + n: v for n, v in arrays.items()}], core_ids=[0])
    return result.results[0]["out_dram"].reshape(1, BLOCKS * P, D)
```
